# Optimizing a Trainium2 kernel written in Bass

```python
import jax, jax.numpy as jnp
from jax import lax
import numpy as np
import math

D_MODEL = 1024
BATCH = 1
SEQ = 512
DEPTH = 2

CHUNK = 64
N_A_LAYERS = DEPTH // 2
N_B_LAYERS = DEPTH - N_A_LAYERS
A_HEADS = 8
A_DQK = D_MODEL // 16
A_DV = D_MODEL // 8
A_QK = A_HEADS * A_DQK
A_V = A_HEADS * A_DV
A_IN = 2 * A_QK + 2 * A_V + 2 * A_HEADS
B_HEADS = 16
B_DH = D_MODEL // B_HEADS
B_DIM = B_HEADS * B_DH
LEFT_CHUNKS = 8
BAND = (LEFT_CHUNKS + 1) * CHUNK
MAX_REL = 256
N_REL = 2 * MAX_REL + 1
D_FF = -(-8 * D_MODEL // (3 * 256)) * 256
EPS = 1e-6
NEG_INIT = -1e30


def rmsnorm(x, g):
    x32 = x.astype(jnp.float32)
    y = x32 * lax.rsqrt(jnp.mean(x32 * x32, axis=-1, keepdims=True) + EPS) * g.astype(jnp.float32)
    return y.astype(x.dtype)

def swiglu(h, w_gate, w_up, w_down):
    return (jax.nn.silu(h @ w_gate) * (h @ w_up)) @ w_down

def mlstm_mixer(h, w_in, b_gate, g_head, w_out):
    B, S, _ = h.shape
    nc = S // CHUNK
    proj = h @ w_in
    q = proj[..., :A_QK].astype(jnp.float32).reshape(B, S, A_HEADS, A_DQK)
    k = proj[..., A_QK:2 * A_QK].astype(jnp.float32).reshape(B, S, A_HEADS, A_DQK) * (A_DQK ** -0.5)
    v = proj[..., 2 * A_QK:2 * A_QK + A_V].astype(jnp.float32).reshape(B, S, A_HEADS, A_DV)
    o_pre = proj[..., 2 * A_QK + A_V:2 * A_QK + 2 * A_V]
    gates = proj[..., 2 * A_QK + 2 * A_V:].astype(jnp.float32) + b_gate.astype(jnp.float32)
    i_log = gates[..., :A_HEADS]
    f_log = jax.nn.log_sigmoid(gates[..., A_HEADS:])

    def to_chunks(t):
        return t.reshape(B, nc, CHUNK, A_HEADS, -1).transpose(1, 0, 3, 2, 4)

    def gate_chunks(t):
        return t.reshape(B, nc, CHUNK, A_HEADS).transpose(1, 0, 3, 2)

    tri = jnp.tril(jnp.ones((CHUNK, CHUNK), dtype=bool))

    def step(carry, xs):
        C, n, m = carry
        qc, kc, vc, ic, fc = xs
        b = jnp.cumsum(fc, axis=-1)
        logD = b[..., :, None] - b[..., None, :] + ic[..., None, :]
        logD = jnp.where(tri, logD, -jnp.inf)
        inter = b + m[..., None]
        m_j = jnp.maximum(inter, jnp.max(logD, axis=-1))
        D = jnp.exp(logD - m_j[..., None])
        w_inter = jnp.exp(inter - m_j)
        s = jnp.einsum('bhld,bhsd->bhls', qc, kc) * D
        num = jnp.einsum('bhls,bhsv->bhlv', s, vc) + w_inter[..., None] * jnp.einsum('bhvd,bhld->bhlv', C, qc)
        den = jnp.sum(s, axis=-1) + w_inter * jnp.einsum('bhd,bhld->bhl', n, qc)
        h_out = num / jnp.maximum(jnp.abs(den), jnp.exp(-m_j))[..., None]
        bL = b[..., -1]
        a = bL[..., None] - b + ic
        m_new = jnp.maximum(bL + m, jnp.max(a, axis=-1))
        wa = jnp.exp(a - m_new[..., None])
        decay = jnp.exp(bL + m - m_new)
        C_new = decay[..., None, None] * C + jnp.einsum('bhs,bhsv,bhsd->bhvd', wa, vc, kc)
        n_new = decay[..., None] * n + jnp.einsum('bhs,bhsd->bhd', wa, kc)
        return (C_new, n_new, m_new), h_out

    init = (jnp.zeros((B, A_HEADS, A_DV, A_DQK), jnp.float32),
            jnp.zeros((B, A_HEADS, A_DQK), jnp.float32),
            jnp.full((B, A_HEADS), NEG_INIT, jnp.float32))
    _, hs = lax.scan(step, init, (to_chunks(q), to_chunks(k), to_chunks(v),
                                  gate_chunks(i_log), gate_chunks(f_log)))
    hs = hs.transpose(1, 0, 3, 2, 4).reshape(B, S, A_HEADS, A_DV)
    hs = hs * lax.rsqrt(jnp.mean(hs * hs, axis=-1, keepdims=True) + EPS)
    hs = hs.reshape(B, S, A_V) * g_head.astype(jnp.float32)
    hs = jax.nn.sigmoid(o_pre.astype(jnp.float32)) * hs
    return hs.astype(h.dtype) @ w_out

def chunked_relpos_attention(h, w_q, rel_table, w_o, k_sh, v_sh):
    B, S, _ = h.shape
    nc = S // CHUNK
    q = (h @ w_q).reshape(B, S, B_HEADS, B_DH) * (B_DH ** -0.5)
    q_chunks = q.reshape(B, nc, CHUNK, B_HEADS, B_DH).transpose(1, 0, 2, 3, 4)
    pad = ((0, 0), (LEFT_CHUNKS * CHUNK, 0), (0, 0), (0, 0))
    k_pad = jnp.pad(k_sh, pad)
    v_pad = jnp.pad(v_sh, pad)
    qi = jnp.arange(CHUNK)[:, None]
    kj = jnp.arange(BAND)[None, :]
    dist = LEFT_CHUNKS * CHUNK + qi - kj
    rel_idx = jnp.clip(dist, -MAX_REL, MAX_REL) + MAX_REL
    bias = rel_table.astype(jnp.float32)[:, rel_idx]

    def one_chunk(args):
        c, qc = args
        start = c * CHUNK
        kb = lax.dynamic_slice_in_dim(k_pad, start, BAND, axis=1)
        vb = lax.dynamic_slice_in_dim(v_pad, start, BAND, axis=1)
        s = jnp.einsum('bqhd,bkhd->bhqk', qc, kb).astype(jnp.float32) + bias
        valid = (start - LEFT_CHUNKS * CHUNK + jnp.arange(BAND)) >= 0
        s = jnp.where(valid, s, -jnp.inf)
        p = jax.nn.softmax(s, axis=-1)
        return jnp.einsum('bhqk,bkhd->bqhd', p.astype(vb.dtype), vb)

    out = lax.map(one_chunk, (jnp.arange(nc), q_chunks))
    out = out.transpose(1, 0, 2, 3, 4).reshape(B, S, B_DIM)
    return out @ w_o

def first_inputs(seed: int = 0) -> dict:
    key = jax.random.key(seed)
    ks = jax.random.split(key, 20)
    nrm = jax.random.normal
    f32 = jnp.float32
    x = nrm(ks[0], (BATCH, SEQ, D_MODEL), f32)
    a_w_in = nrm(ks[1], (N_A_LAYERS, D_MODEL, A_IN), f32) * D_MODEL ** -0.5
    a_b_gate = jnp.concatenate([0.1 * nrm(ks[2], (N_A_LAYERS, A_HEADS), f32),
                                3.0 + 0.5 * nrm(ks[3], (N_A_LAYERS, A_HEADS), f32)], axis=-1)
    a_g_head = 1.0 + 0.05 * nrm(ks[4], (N_A_LAYERS, A_V), f32)
    a_w_out = nrm(ks[5], (N_A_LAYERS, A_V, D_MODEL), f32) * A_V ** -0.5
    b_w_q = nrm(ks[6], (N_B_LAYERS, D_MODEL, B_DIM), f32) * D_MODEL ** -0.5
    b_rel_bias = 0.1 * nrm(ks[7], (N_B_LAYERS, B_HEADS, N_REL), f32)
    b_w_o = nrm(ks[8], (N_B_LAYERS, B_DIM, D_MODEL), f32) * B_DIM ** -0.5
    kv_norm_g = 1.0 + 0.05 * nrm(ks[9], (D_MODEL,), f32)
    w_kv = nrm(ks[10], (D_MODEL, 2 * B_DIM), f32) * D_MODEL ** -0.5
    norm_mix_g = 1.0 + 0.05 * nrm(ks[11], (DEPTH, D_MODEL), f32)
    norm_ffn_g = 1.0 + 0.05 * nrm(ks[12], (DEPTH, D_MODEL), f32)
    ffn_w_gate = nrm(ks[13], (DEPTH, D_MODEL, D_FF), f32) * D_MODEL ** -0.5
    ffn_w_up = nrm(ks[14], (DEPTH, D_MODEL, D_FF), f32) * D_MODEL ** -0.5
    ffn_w_down = nrm(ks[15], (DEPTH, D_FF, D_MODEL), f32) * D_FF ** -0.5
    final_norm_g = 1.0 + 0.05 * nrm(ks[16], (D_MODEL,), f32)
    return {"x": x, "a_w_in": a_w_in, "a_b_gate": a_b_gate, "a_g_head": a_g_head,
            "a_w_out": a_w_out, "b_w_q": b_w_q, "b_rel_bias": b_rel_bias, "b_w_o": b_w_o,
            "kv_norm_g": kv_norm_g, "w_kv": w_kv, "norm_mix_g": norm_mix_g,
            "norm_ffn_g": norm_ffn_g, "ffn_w_gate": ffn_w_gate, "ffn_w_up": ffn_w_up,
            "ffn_w_down": ffn_w_down, "final_norm_g": final_norm_g}

def first_block(x, a_w_in, a_b_gate, a_g_head, a_w_out, b_w_q, b_rel_bias, b_w_o,
              kv_norm_g, w_kv, norm_mix_g, norm_ffn_g, ffn_w_gate, ffn_w_up,
              ffn_w_down, final_norm_g):
    B, S, _ = x.shape
    h = x
    k_sh = None
    v_sh = None
    for l in range(DEPTH):
        if l == N_A_LAYERS:
            kv = rmsnorm(h, kv_norm_g) @ w_kv
            k_sh = kv[..., :B_DIM].reshape(B, S, B_HEADS, B_DH)
            v_sh = kv[..., B_DIM:].reshape(B, S, B_HEADS, B_DH)
        hn = rmsnorm(h, norm_mix_g[l])
        if l < N_A_LAYERS:
            h = h + mlstm_mixer(hn, a_w_in[l], a_b_gate[l], a_g_head[l], a_w_out[l])
        else:
            j = l - N_A_LAYERS
            h = h + chunked_relpos_attention(hn, b_w_q[j], b_rel_bias[j], b_w_o[j], k_sh, v_sh)
        h = h + swiglu(rmsnorm(h, norm_ffn_g[l]), ffn_w_gate[l], ffn_w_up[l], ffn_w_down[l])
    return rmsnorm(h, final_norm_g)


DEPTH_2 = 1

HEAD_DIM = 64
DA_HEADS = 4
DA_QK = DA_HEADS * 2 * HEAD_DIM
DA_V = DA_HEADS * 2 * HEAD_DIM
NA_HEADS = 8
NA_W = NA_HEADS * HEAD_DIM
GRID_W = 64
NA_ROWS = 8
NA_COLS = 16
Q_BLOCK = 128
D_FF_2 = int(math.ceil(8 * D_MODEL / 3 / 256) * 256)
IN_COLS = 2 * DA_QK + DA_V + 3 * NA_W + 2 * D_MODEL
NEG = -1e30


def rmsnorm_2(x, w):
    xf = x.astype(jnp.float32)
    y = xf * lax.rsqrt(jnp.mean(xf * xf, axis=-1, keepdims=True) + EPS)
    return (y * w.astype(jnp.float32)).astype(x.dtype)

def alibi_slopes(n):
    return jnp.asarray([2.0 ** (-8.0 * (i + 1) / n) for i in range(n)], dtype=jnp.float32)

def diff_attention(q, k, v, lam, subln_w, lambda_init):
    B, S, H, _, d = q.shape
    nb = S // Q_BLOCK
    scale = d ** -0.5
    slopes = alibi_slopes(H)
    kpos = jnp.arange(S)
    qb = jnp.moveaxis(q.reshape(B, nb, Q_BLOCK, H, 2, d), 1, 0)

    def block(args):
        qi, i = args
        s = jnp.einsum('bqhcd,bkhcd->bhcqk', qi, k).astype(jnp.float32) * scale
        qpos = i * Q_BLOCK + jnp.arange(Q_BLOCK)
        dist = jnp.abs(qpos[:, None] - kpos[None, :]).astype(jnp.float32)
        s = s - slopes[None, :, None, None, None] * dist[None, None, None]
        p = jax.nn.softmax(s, axis=-1)
        a = p[:, :, 0] - lam * p[:, :, 1]
        return jnp.einsum('bhqk,bkhe->bqhe', a.astype(v.dtype), v)

    o = lax.map(block, (qb, jnp.arange(nb)))
    o = jnp.moveaxis(o, 0, 1).reshape(B, S, H, 2 * d)
    o = rmsnorm_2(o, subln_w) * (1.0 - lambda_init)
    return o.reshape(B, S, H * 2 * d)

def neighbourhood_attention_2d(q, k, v, rpb):
    B, S, H, d = q.shape
    rows = S // GRID_W
    kr = min(NA_ROWS, rows)
    kc = NA_COLS
    scale = d ** -0.5
    qg = q.reshape(B, rows, GRID_W, H, d)
    kg = k.reshape(B, rows, GRID_W, H, d)
    vg = v.reshape(B, rows, GRID_W, H, d)
    col = jnp.arange(GRID_W)
    col_start = jnp.clip(col - kc // 2, 0, GRID_W - kc)
    col_in = (col[None, :] >= col_start[:, None]) & (col[None, :] < col_start[:, None] + kc)
    col_off = jnp.clip(col[None, :] - col[:, None] + NA_COLS - 1, 0, 2 * NA_COLS - 2)
    rpb_cols = rpb[:, :, col_off]

    def row_step(args):
        qr, r = args
        rs = jnp.clip(r - kr // 2, 0, rows - kr)
        kb = lax.dynamic_slice_in_dim(kg, rs, kr, axis=1)
        vb = lax.dynamic_slice_in_dim(vg, rs, kr, axis=1)
        s = jnp.einsum('bqhd,bikhd->bhqik', qr, kb).astype(jnp.float32) * scale
        row_off = rs + jnp.arange(kr) - r + NA_ROWS - 1
        bias = jnp.transpose(rpb_cols[:, row_off], (0, 2, 1, 3))
        s = s + bias[None].astype(jnp.float32)
        s = jnp.where(col_in[None, None, :, None, :], s, NEG)
        p = jax.nn.softmax(s, axis=(-2, -1))
        return jnp.einsum('bhqik,bikhd->bqhd', p.astype(v.dtype), vb)

    o = lax.map(row_step, (jnp.moveaxis(qg, 1, 0), jnp.arange(rows)))
    return jnp.moveaxis(o, 0, 1).reshape(B, S, H * d)

def second_inputs(seed: int = 0) -> dict:
    key = jax.random.key(seed)
    ks = jax.random.split(key, 24)
    f32 = jnp.float32

    def nrm(k, shape, scale):
        return jax.random.normal(k, shape, f32) * scale

    def gain(k):
        return 1.0 + nrm(k, (DEPTH_2, D_MODEL), 0.02)

    return {
        "x": nrm(ks[0], (BATCH, SEQ, D_MODEL), 1.0),
        "pre_mix_w": gain(ks[1]),
        "w_in": nrm(ks[2], (DEPTH_2, D_MODEL, IN_COLS), D_MODEL ** -0.5),
        "b_gate": nrm(ks[3], (DEPTH_2, 2 * D_MODEL), 0.1),
        "lambda_q1": nrm(ks[4], (DEPTH_2, HEAD_DIM), 0.1),
        "lambda_k1": nrm(ks[5], (DEPTH_2, HEAD_DIM), 0.1),
        "lambda_q2": nrm(ks[6], (DEPTH_2, HEAD_DIM), 0.1),
        "lambda_k2": nrm(ks[7], (DEPTH_2, HEAD_DIM), 0.1),
        "subln_w": 1.0 + nrm(ks[8], (DEPTH_2, 2 * HEAD_DIM), 0.02),
        "rpb": nrm(ks[9], (DEPTH_2, NA_HEADS, 2 * NA_ROWS - 1, 2 * NA_COLS - 1), 0.1),
        "w_branch_a": nrm(ks[10], (DEPTH_2, DA_V, D_MODEL), DA_V ** -0.5),
        "w_branch_b": nrm(ks[11], (DEPTH_2, NA_W, D_MODEL), NA_W ** -0.5),
        "w_out": nrm(ks[12], (DEPTH_2, D_MODEL, D_MODEL), D_MODEL ** -0.5),
        "post_mix_w": gain(ks[13]),
        "pre_ffn_w": gain(ks[14]),
        "w_gate": nrm(ks[15], (DEPTH_2, D_MODEL, D_FF_2), D_MODEL ** -0.5),
        "w_up": nrm(ks[16], (DEPTH_2, D_MODEL, D_FF_2), D_MODEL ** -0.5),
        "w_down": nrm(ks[17], (DEPTH_2, D_FF_2, D_MODEL), D_FF_2 ** -0.5),
        "post_ffn_w": gain(ks[18]),
    }

def second_block(x, pre_mix_w, w_in, b_gate, lambda_q1, lambda_k1, lambda_q2, lambda_k2,
              subln_w, rpb, w_branch_a, w_branch_b, w_out, post_mix_w, pre_ffn_w,
              w_gate, w_up, w_down, post_ffn_w):
    B, S, _ = x.shape
    for l in range(DEPTH_2):
        lambda_init = 0.8 - 0.6 * math.exp(-0.3 * l)
        h = rmsnorm_2(x, pre_mix_w[l])
        proj = h @ w_in[l]
        o0 = 0
        q_a = proj[..., o0:o0 + DA_QK].reshape(B, S, DA_HEADS, 2, HEAD_DIM); o0 += DA_QK
        k_a = proj[..., o0:o0 + DA_QK].reshape(B, S, DA_HEADS, 2, HEAD_DIM); o0 += DA_QK
        v_a = proj[..., o0:o0 + DA_V].reshape(B, S, DA_HEADS, 2 * HEAD_DIM); o0 += DA_V
        q_b = proj[..., o0:o0 + NA_W].reshape(B, S, NA_HEADS, HEAD_DIM); o0 += NA_W
        k_b = proj[..., o0:o0 + NA_W].reshape(B, S, NA_HEADS, HEAD_DIM); o0 += NA_W
        v_b = proj[..., o0:o0 + NA_W].reshape(B, S, NA_HEADS, HEAD_DIM); o0 += NA_W
        gates = jax.nn.sigmoid(proj[..., o0:] + b_gate[l])
        g_a, g_b = gates[..., :D_MODEL], gates[..., D_MODEL:]

        lq1 = lambda_q1[l].astype(jnp.float32); lk1 = lambda_k1[l].astype(jnp.float32)
        lq2 = lambda_q2[l].astype(jnp.float32); lk2 = lambda_k2[l].astype(jnp.float32)
        lam = jnp.exp(jnp.sum(lq1 * lk1)) - jnp.exp(jnp.sum(lq2 * lk2)) + lambda_init

        y_a = diff_attention(q_a, k_a, v_a, lam, subln_w[l], lambda_init)
        y_b = neighbourhood_attention_2d(q_b, k_b, v_b, rpb[l])
        merged = g_a * (y_a @ w_branch_a[l]) + g_b * (y_b @ w_branch_b[l])
        x = x + rmsnorm_2(merged @ w_out[l], post_mix_w[l])
        h = rmsnorm_2(x, pre_ffn_w[l])
        f = (jax.nn.silu(h @ w_gate[l]) * (h @ w_up[l])) @ w_down[l]
        x = x + rmsnorm_2(f, post_ffn_w[l])
    return x


def setup_inputs(seed=0):
    out = dict(first_inputs(seed))
    for name, value in second_inputs(seed + 1).items():
        if name != "x":
            out[name + "_2"] = value
    return out


def reference(
    x, a_w_in, a_b_gate, a_g_head, a_w_out, b_w_q, b_rel_bias, b_w_o, kv_norm_g, w_kv,
    norm_mix_g, norm_ffn_g, ffn_w_gate, ffn_w_up, ffn_w_down, final_norm_g, pre_mix_w_2, w_in_2,
    b_gate_2, lambda_q1_2, lambda_k1_2, lambda_q2_2, lambda_k2_2, subln_w_2, rpb_2,
    w_branch_a_2, w_branch_b_2, w_out_2, post_mix_w_2, pre_ffn_w_2, w_gate_2, w_up_2, w_down_2,
    post_ffn_w_2,
):
    x = first_block(
        x, a_w_in, a_b_gate, a_g_head, a_w_out, b_w_q, b_rel_bias, b_w_o, kv_norm_g, w_kv,
        norm_mix_g, norm_ffn_g, ffn_w_gate, ffn_w_up, ffn_w_down, final_norm_g,
    )
    return second_block(
        x, pre_mix_w_2, w_in_2, b_gate_2, lambda_q1_2, lambda_k1_2, lambda_q2_2, lambda_k2_2,
        subln_w_2, rpb_2, w_branch_a_2, w_branch_b_2, w_out_2, post_mix_w_2, pre_ffn_w_2,
        w_gate_2, w_up_2, w_down_2, post_ffn_w_2,
    )


_drawn_inputs = setup_inputs


def setup_inputs(seed=0):
    import zlib

    import numpy as np

    out = dict(_drawn_inputs(seed))
    spreads = {}
    factors = {'b_rel_bias': 3.807,
     'kv_norm_g': 3.245,
     'lambda_q1_2': 8.0,
     'subln_w_2': 3.631,
     'rpb_2': 4.007,
     'post_mix_w_2': 3.373,
     'pre_ffn_w_2': 3.435,
     'post_ffn_w_2': 4.84}
    for name, (base, spread) in spreads.items():
        noise = np.random.default_rng([zlib.crc32(name.encode()), seed]).standard_normal(out[name].shape)
        drawn = base * np.exp(spread * noise) if base else spread * noise
        out[name] = __import__('jax').numpy.asarray(drawn.astype(out[name].dtype))
    for name, factor in factors.items():
        out[name] = (out[name] * factor).astype(out[name].dtype)
    return out
```

```python
import math
from contextlib import ExitStack

import concourse.bass as bass
from concourse import mybir

F32 = mybir.dt.float32
F32R = mybir.dt.float32r
ACT = mybir.ActivationFunctionType
ALU = mybir.AluOpType

P = 128
S = 512
D = 1024
DT = D // P
TT = S // P
EPS = 1e-6
CHUNK = 64
A_HEADS, A_DQK, A_DV = 8, 64, 128
B_HEADS, DH = 16, 64
MAX_REL = 256
N_REL = 2 * MAX_REL + 1
DFF = 2816
HALVES = (12, 10)
DA_HEADS = 4
NA_HEADS, NA_ROWS, NA_COLS, GRID_W = 8, 8, 16, 64
NEG = -1e30
LN_EXP = "natural_log_exp_and_others"
LAMBDA_INIT = 0.8 - 0.6 * math.exp(0.0)
SCALE = DH ** -0.5
UP = 1.0 / SCALE
SLOT = 8 * 256

(MIX0, FFN0, KVN, MIX1, FFN1, FINAL, PREMIX, POSTMIX, PREFFN, POSTFFN) = (8 * i for i in range(10))
GHEAD, BGATE2, SUBLN, NGAIN = 80, 88, 104, 105
EXT = 640
RPW = 127
NRO = 14


class Stage:

    def __init__(self, kind, blocks, kt=DT):
        self.kind, self.blocks, self.kt = kind, blocks, kt
        self.elems = {"merge": None, "down": kt * P}.get(kind, SLOT)


def plan():
    st = {}

    def add(name, kind, blocks, kt=DT, squares=False):
        st[name] = Stage(kind, blocks, kt)
        st[name].squares = squares

    add("A_qk", "copy", 4)
    add("A_v", "tokens", 4)
    add("A_o", "sigmoid", 4)
    add("A_out", "residual", 4, squares=True)
    for f in range(3):
        if f == 1:
            add("B_k", "copy", 4)
            add("B_v", "tokens", 4)
            add("B_q", "copy", 4)
            add("B_out", "residual", 4, squares=True)
        if f == 2:
            add("C_qka", "copy", 4)
            add("C_va", "tokens", 2)
            add("C_qkb", "copy", 4)
            add("C_vb", "tokens", 2)
            add("C_merge", "merge", 16)
            add("C_out", "store", 4, squares=True)
        for half, kt in enumerate(HALVES):
            add(f"up{f}{half}", "up", kt)
            add(f"down{f}{half}", "down", 8, kt=kt, squares=(half == 1))
    b = h = r = m = s = 0
    order = list(st.values())
    for x in order:
        assert x.blocks % 2 == 0
        x.b0, x.h0, x.r0, x.m0, x.s0 = b, h, r, m, s
        b += x.blocks
        h += x.blocks if x.kind == "up" else 0
        r += DT if x.squares else 0
        m += x.blocks // 2 if x.kind == "merge" else 0
        s += DT if x.kind in ("residual", "down", "store") else 0
    for x, y in zip(order, order[1:] + [None]):
        x.next = y
    return st


def weights_of(stage, par):
    if stage.kind == "merge":
        return SLOT if par == 0 else SLOT // 2
    return stage.kt * P if stage.kind == "down" else SLOT


class Rows:

    def __init__(self, heads, maps, causal, per_tile, lag):
        self.heads, self.maps, self.causal, self.per_tile, self.lag = heads, maps, causal, per_tile, lag
        self.units = heads * TT

    def keys(self, qt):
        return (qt + 1) * P if self.causal else S


def attentions():
    a = {"B": Rows(B_HEADS, 1, True, 2, 2), "DA": Rows(DA_HEADS, 2, False, 1, 1), "NA": Rows(NA_HEADS, 1, False, 2, 2)}
    s = u = h = y = i = 0
    for r in a.values():
        r.s0, r.u0, r.p0, r.y0, r.i0 = s, u, h, y, i
        s += r.units * r.maps
        u += r.units
        h += r.heads
        y += r.heads // r.per_tile
        i += r.units * (1 if r.maps == 1 else 3)
    return a


def build(nc, x, a_w_in, a_b_gate, a_g_head, a_w_out, b_w_q, b_rel_bias, b_w_o, kv_norm_g, w_kv,
          norm_mix_g, norm_ffn_g, ffn_w_gate, ffn_w_up, ffn_w_down, final_norm_g, pre_mix_w, w_in,
          b_gate, lambda_q1, lambda_k1, lambda_q2, lambda_k2, subln_w, rpb, w_branch_a, w_branch_b,
          w_out, post_mix_w, pre_ffn_w, w_gate, w_up, w_down, post_ffn_w, out):
    st = plan()
    att = attentions()
    with ExitStack() as ctx:
        def sem(name):
            return ctx.enter_context(nc.semaphore(name))

        def sb(name, shape, dt=F32):
            return ctx.enter_context(nc.sbuf_tensor(name, shape, dt))

        ident = sb("ident", [P, P])
        ones = sb("ones", [P, P])
        gains = sb("gains", [P, NGAIN])
        ss = sb("ss", [P, S])
        rs = sb("rs", [P, S])
        rowmax = sb("rowmax", [P, P])
        rowsum = sb("rowsum", [P, P])
        rowinv = sb("rowinv", [P, P])
        lam = sb("lam", [P, 8])
        namask = sb("namask", [P, GRID_W])
        eps = sb("eps", [P, 2])
        stage = sb("stage", [P, 2, SLOT])
        wh = sb("wh", [P, 2, SLOT], F32R)
        wl = sb("wl", [P, 2, SLOT], F32R)
        res = sb("res", [P, DT, S])
        xh = sb("xh", [P, DT, S], F32R)
        xl = sb("xl", [P, DT, S], F32R)
        KB = 1024
        region_base = nc.sbuf_base
        sb("region", [P, 104 * KB // 4])

        def at(name, kb, shape, dt=F32):
            return nc.alloc_sbuf_tensor_at(name, shape, dt, offset=region_base + int(kb * KB))

        work = at("work", 64, [P, 4, S])
        hidh = at("hidh", 0, [P, 12, S], F32R)
        hidl = at("hidl", 24, [P, 12, S], F32R)
        acc = at("acc", 48, [P, DT, S])
        xin = at("xin", 0, [P, TT, D])
        extsrc = at("extsrc", 48, [B_HEADS, N_REL])
        ext = at("ext", 51, [B_HEADS, EXT])
        rpsrc = at("rpsrc", 54, [NA_HEADS * 15, 31])
        rppad = at("rppad", 55, [NA_HEADS * 15, RPW])
        gload = at("gload", 72, [P, P])
        lrow = at("lrow", 102.5, [1, 4, DH])
        qk = at("qk", 0, [P, DT, S])
        va = at("va", 16, [P, TT, D])
        og = at("og", 32, [P, DT, S])
        pt = at("pt", 48, [P, 2, 4, S])
        wg = at("wg", 73, [P, DT, 16])
        wgh = at("wgh", 74, [P, DT, 16], F32R)
        wgl = at("wgl", 75, [P, DT, 16], F32R)
        gi = at("gi", 76, [16, S])
        gf = at("gf", 78, [A_HEADS, S])
        lf = at("lf", 80, [A_HEADS, S])
        gb = at("gb", 82, [A_HEADS, S])
        gu = at("gu", 84, [A_HEADS, S])
        gm = at("gm", 86, [A_HEADS, S])
        gn = at("gn", 88, [A_HEADS, S])
        sel = at("sel", 90, [A_HEADS, A_HEADS, P])
        ut = at("ut", 94, [P, TT, A_HEADS])
        efl = at("efl", 94.25, [P, 2, S])
        hs = at("hs", 98.25, [P, S])
        hq = at("hq", 100.25, [P, S])
        dn = at("dn", 76, [P, S])
        hr = at("hr", 78, [P, S])
        hn = at("hn", 80, [P, S])
        brow = at("brow", 102.25, [16, 1])
        bk = at("bk", 0, [P, DT, S])
        bv = at("bv", 16, [P, TT, D])
        bq = at("bq", 32, [P, DT, S])
        relt = at("relt", 72, [P, B_HEADS, S])
        cva = at("cva", 16, [P, TT, 512])
        qkb = at("qkb", 24, [P, DT, S])
        cvb = at("cvb", 40, [P, TT, 512])
        rpt = at("rpt", 72, [P, 2, NRO, GRID_W])
        datmp = at("datmp", 80, [P, 2, S])
        absd = at("absd", 84, [P, 896])
        yah = at("yah", 88, [P, 4, S], F32R)
        yal = at("yal", 96, [P, 4, S], F32R)
        ybh = at("ybh", 0, [P, 4, S], F32R)
        ybl = at("ybl", 8, [P, 4, S], F32R)
        mgh = at("mgh", 16, [P, DT, S], F32R)
        mgl = at("mgl", 32, [P, DT, S], F32R)

        psum = ctx.enter_context(nc.psum_tensor("psum", [P, 8, S], F32))
        ext_dram = nc.dram_tensor("ext_scratch", [B_HEADS, EXT], F32, kind="Internal").ap()
        rp_dram = nc.dram_tensor("rp_scratch", [NA_HEADS * 15, RPW], F32, kind="Internal").ap()

        w_loaded = [sem("w_loaded0"), sem("w_loaded1")]
        w_hi, w_lo = sem("w_hi"), sem("w_lo")
        mm_done = sem("mm_done")
        block_out = sem("block_out")
        n_full, n_hi, n_lo = sem("n_full"), sem("n_hi"), sem("n_lo")
        norm_sum = sem("norm_sum")
        norm_root, norm_rs, ss_zero = sem("norm_root"), sem("norm_rs"), sem("ss_zero")
        sq_src, tile_sq, ss_added = sem("sq_src"), sem("tile_sq"), sem("ss_added")
        h_sig, h_act, h_hi, h_lo = sem("h_sig"), sem("h_act"), sem("h_hi"), sem("h_lo")
        m_a, m_sum, m_hi, m_lo = sem("m_a"), sem("m_sum"), sem("m_hi"), sem("m_lo")
        x_in, small_in, gate_in = sem("x_in"), sem("small_in"), sem("gate_in")
        tab_in, tab_step, tab_out = sem("tab_in"), sem("tab_step"), sem("tab_out")
        relt_in, relt_ready = sem("relt_in"), sem("relt_ready")
        rpt_in, rpt_ready = [sem("rpt_in0"), sem("rpt_in1")], sem("rpt_ready")
        const = sem("const")
        gain_t, gain_out, gain_ready = sem("gain_t"), sem("gain_out"), sem("gain_ready")
        xt_done, xt_out = sem("xt_done"), sem("xt_out")
        wg_hi, wg_lo, g_done, g_step, g_act = sem("wg_hi"), sem("wg_lo"), sem("g_done"), sem("g_step"), sem("g_act")
        gf_in, u_t, u_ready = sem("gf_in"), sem("u_t"), sem("u_ready")
        lam_step, lam_exp, lam_mm = sem("lam_step"), sem("lam_exp"), sem("lam_mm")
        a_mrow, a_floor, a_s, a_d, a_mask, a_p = (sem(n) for n in ("a_mrow", "a_floor", "a_s", "a_d", "a_mask", "a_p"))
        a_den, a_abs, a_step, a_sq, a_ss, a_ln, a_rs, a_gated, a_hi, a_lo = (
            sem(n) for n in ("a_den", "a_abs", "a_step", "a_sq", "a_ss", "a_ln", "a_rs", "a_gated", "a_hi", "a_lo"))
        s_done, s_biased, s_exp, s_inv, s_prob = (sem(n) for n in ("s_done", "s_biased", "s_exp", "s_inv", "s_prob"))
        t_done, t_out, pv_done, y_hi, y_lo = (sem(n) for n in ("t_done", "t_out", "pv_done", "y_hi", "y_lo"))
        d_sq, d_ss, d_ln, d_rs, d_full, absd_ready, absd_scaled = (
            sem(n) for n in ("d_sq", "d_ss", "d_ln", "d_rs", "d_full", "absd_ready", "absd_scaled"))
        post_scaled, ot_done, ot_out, stored = sem("post_scaled"), sem("ot_done"), sem("ot_out"), sem("stored")

        EVENT = {"x": 0, "A_out": 1, "down01": 2, "B_out": 3, "down11": 4, "final": 5, "C_out": 6,
                 "post_mix": 7, "down21": 8}

        block = ctx.enter_context(nc.Block())

        def run_pairs(eng, stage_, step):
            n = stage_.blocks // 2 - 1
            if n > 1 and stage_.b0:
                with eng.Fori(0, n) as j:
                    step(j, 0)
                    step(j, 1)
            else:
                for j in range(n):
                    step(j, 0)
                    step(j, 1)

        @block.sync
        def _(sp):
            def sources(name, i):
                s = st[name]

                def cols(w, c, n):
                    return w[:, bass.ds(c, n)].rearrange("(k p) n -> p k n", p=P)

                if s.kind == "up":
                    f = int(name[2])
                    g = ffn_w_gate[f] if f < 2 else w_gate[0]
                    u = ffn_w_up[f] if f < 2 else w_up[0]
                    c = HALVES[0] * P * int(name[3])
                    return [cols(g, i * P + c, P), cols(u, i * P + c, P)], (DT, P)
                if s.kind == "down":
                    f, half = int(name[4]), int(name[5])
                    w = ffn_w_down[f] if f < 2 else w_down[0]
                    r, k = HALVES[0] * P * half, s.kt // 2 * P
                    return [cols(w[r:r + k, :], i * P, P), cols(w[r + k:r + 2 * k, :], i * P, P)], (s.kt // 2, P)
                w, c = {"A_qk": (a_w_in[0], 0), "A_v": (a_w_in[0], 1024), "A_o": (a_w_in[0], 2048),
                        "A_out": (a_w_out[0], 0), "B_k": (w_kv, 0), "B_v": (w_kv, 1024), "B_q": (b_w_q[0], 0),
                        "B_out": (b_w_o[0], 0), "C_qka": (w_in[0], 0), "C_va": (w_in[0], 1024),
                        "C_qkb": (w_in[0], 1536), "C_vb": (w_in[0], 2560), "C_out": (w_out[0], 0)}[name]
                k = DT // 2 * P
                return [cols(w[0:k, :], i * 256 + c, 256), cols(w[k:2 * k, :], i * 256 + c, 256)], (DT // 2, 256)

            def merge_sources(j, par):
                def cols(w, c):
                    return w[:, bass.ds(c, P)].rearrange("(k p) n -> p k n", p=P)

                if par == 0:
                    return [cols(w_in[0], j * P + 3072), cols(w_in[0], j * P + 4096)], (DT, P)
                return [cols(w_branch_a[0], j * P), cols(w_branch_b[0], j * P)], (4, P)

            def load(s, name, j, par):
                b = s.b0 + 2 * j + par
                if s.kind == "merge":
                    if par == 0:
                        sp.wait_ge(w_lo, b)
                elif not isinstance(b, int) or b >= 2:
                    sp.wait_ge(w_lo, b - 1)
                src, (k, n) = merge_sources(j, par) if s.kind == "merge" else sources(name, 2 * j + par)
                dst = stage[:, par, 0:2 * k * n].rearrange("p (a k n) -> p a k n", a=2, k=k)
                for a in range(2):
                    sp.dma_start(dst[:, a], src[a]).then_inc(w_loaded[par], 16)

            def load_neighbour_biases():
                for h in range(NA_HEADS):
                    if h < 2:
                        sp.wait_ge(s_biased, att["DA"].s0)
                    else:
                        sp.wait_ge(s_biased, att["NA"].s0 + TT * (h - 1))
                    for half in range(2):
                        src = bass.AP(rp_dram.tensor, (15 * h + 1 - half) * RPW,
                                      [[1, GRID_W], [RPW, NRO], [1, GRID_W]])
                        sp.dma_start(rpt[64 * half:64 * half + 64, h % 2], src).then_inc(rpt_in[h % 2], 16)

            def load_stage(name):
                s = st[name]
                if s.kind == "merge":
                    load(s, name, 0, 0)
                    load(s, name, 0, 1)
                    load_neighbour_biases()
                    with nc.sync.Fori(1, s.blocks // 2) as j:
                        load(s, name, j, 0)
                        load(s, name, j, 1)
                    return
                if s.b0 == 0 or s.blocks == 2:
                    for j in range(s.blocks // 2):
                        load(s, name, j, 0)
                        load(s, name, j, 1)
                else:
                    with nc.sync.Fori(0, s.blocks // 2) as j:
                        load(s, name, j, 0)
                        load(s, name, j, 1)

            for t in range(TT):
                sp.dma_start(xin[:, t, :], x[0, t * P:(t + 1) * P, :]).then_inc(x_in, 16)
            vectors = [(MIX0, norm_mix_g[0]), (FFN0, norm_ffn_g[0]), (KVN, kv_norm_g), (MIX1, norm_mix_g[1]),
                       (FFN1, norm_ffn_g[1]), (FINAL, final_norm_g), (PREMIX, pre_mix_w[0]),
                       (POSTMIX, post_mix_w[0]), (PREFFN, pre_ffn_w[0]), (POSTFFN, post_ffn_w[0]),
                       (GHEAD, a_g_head[0]), (BGATE2, b_gate[0]), (SUBLN, subln_w[0])]
            for row, v in vectors:
                n = v.shape[0] // P
                sp.dma_start(gload[row:row + n, :], v.rearrange("(a b) -> a b", b=P)).then_inc(small_in, 16)
            sp.dma_start(brow[:, :], a_b_gate[0].rearrange("(a b) -> a b", b=1)).then_inc(small_in, 16)
            for i, v in enumerate((lambda_q1, lambda_k1, lambda_q2, lambda_k2)):
                sp.dma_start(lrow[0:1, i, :], v).then_inc(small_in, 16)
            sp.dma_start(wg[:, :, :], a_w_in[0, :, 3072:3088].rearrange("(k p) n -> p k n", p=P)).then_inc(gate_in, 16)
            sp.dma_start(extsrc[:, :], b_rel_bias[0]).then_inc(tab_in, 16)
            sp.dma_start(rpsrc[:, :], rpb[0].rearrange("h a b -> (h a) b")).then_inc(tab_in, 16)
            load(st["A_qk"], "A_qk", 0, 0)
            load(st["A_qk"], "A_qk", 0, 1)
            sp.wait_ge(tab_step, 3)
            sp.dma_start(ext_dram, ext[:, :]).then_inc(tab_out, 16)
            sp.dma_start(rp_dram, rppad[:, :]).then_inc(tab_out, 16)
            sp.wait_ge(tab_out, 32)
            load(st["A_qk"], "A_qk", 1, 0)
            load(st["A_qk"], "A_qk", 1, 1)

            for name in list(st)[1:]:
                load_stage(name)
                if name == "A_out":
                    sp.wait_ge(a_lo, A_HEADS)
                    src = bass.AP(ext_dram.tensor, 0, [[1, P], [EXT, B_HEADS], [1, S]])
                    sp.dma_start(relt[:, :, :], src).then_inc(relt_in, 16)
            out_t = out[0].rearrange("(t p) d -> p t d", p=P)
            for t in range(TT):
                sp.wait_ge(ot_out, 2 * (t + 1))
                sp.dma_start(out_t[:, t, :], acc[:, 2 * t:2 * t + 2, :].rearrange("p a b -> p (a b)")).then_inc(stored, 16)
            sp.wait_ge(stored, 16 * TT)

        @block.gpsimd
        def _(pool):
            nc.gpsimd.memset(ones[:, :], 1.0).then_inc(const, 1)
            nc.gpsimd.memset(sel[:, :, :], 1.0).then_inc(const, 1)
            nc.gpsimd.memset(rppad[:, :], 0.0).then_inc(const, 1)
            nc.gpsimd.memset(namask[:, :], 0.0).then_inc(const, 1)
            nc.gpsimd.memset(eps[:, 0:1], D * EPS).then_inc(const, 1)
            nc.gpsimd.memset(eps[:, 1:2], A_DV * EPS).then_inc(const, 1)
            pool.wait_ge(const, 6)
            nc.gpsimd.affine_select(out=ident[:, :], in_=ones[:, :], compare_op=ALU.is_equal, fill=0.0,
                                    base=0, pattern=[[-1, P]], channel_multiplier=1).then_inc(const, 1)
            nc.gpsimd.affine_select(out=sel[:, :, :], in_=sel[:, :, :], compare_op=ALU.is_equal, fill=0.0,
                                    base=0, pattern=[[-1, A_HEADS], [0, P]], channel_multiplier=1).then_inc(const, 1)
            for half in range(2):
                pool.wait_ge(const, 8 + half)
                m = namask[64 * half:64 * half + 64, 16:64]
                nc.gpsimd.affine_select(out=m, in_=m, compare_op=ALU.is_ge, fill=UP * NEG,
                                        base=GRID_W - 1 - 16 + NA_COLS // 2, pattern=[[-1, 48]],
                                        channel_multiplier=-1).then_inc(const, 1)
            for half in range(2):
                pool.wait_ge(const, 10 + half)
                m = namask[64 * half:64 * half + 64, 0:48]
                nc.gpsimd.affine_select(out=m, in_=m, compare_op=ALU.is_ge, fill=UP * NEG,
                                        base=NA_COLS // 2 - 1 - (GRID_W - 1), pattern=[[1, 48]],
                                        channel_multiplier=1).then_inc(const, 1)
            pool.wait_ge(const, 12)
            for g in range(A_HEADS * TT):
                pool.wait_ge(a_d, g + 1)
                d = work[:, g % TT, 0:P]
                nc.gpsimd.affine_select(out=d, in_=d, compare_op=ALU.is_ge, fill=0.0, base=0,
                                        pattern=[[1, P]], channel_multiplier=-1).then_inc(a_mask, 1)
            pool.wait_ge(relt_in, 16)
            pool.wait_ge(a_mask, A_HEADS * TT)
            nc.gpsimd.memset(relt[0:CHUNK, :, 0:CHUNK], UP * NEG).then_inc(relt_ready, 1)
            pool.wait_ge(relt_ready, 1)
            pool.wait_ge(s_biased, att["DA"].s0)
            nc.gpsimd.iota(absd[:, :], pattern=[[2, 896]], base=-768, channel_multiplier=-2,
                           allow_small_or_imprecise_dtypes=True).then_inc(absd_ready, 1)
            for h in range(NA_HEADS):
                pool.wait_ge(rpt_in[h % 2], 32 * (h // 2 + 1))
                pool.wait_ge(const, 12)
                r = rpt[:, h % 2]
                nc.gpsimd.tensor_tensor(r, r, namask[:, :].unsqueeze(1).to_broadcast([P, NRO, GRID_W]),
                                        ALU.add).then_inc(rpt_ready, 1)

        @block.scalar
        def _(act):
            def split(pair, b, par, n):
                act.wait_ge(w_loaded[par], (pair + 1) * 32)
                if not isinstance(b, int) or b >= 2:
                    act.wait_ge(mm_done, b - 1)
                nc.scalar.copy(wh[:, par, 0:n], stage[:, par, 0:n]).then_inc(w_hi, 1)

            def squares(name, b, i, par):
                two = st[name].kind != "down"
                act.wait_ge(block_out, b + 1)
                for a in range(2 if two else 1):
                    t = 2 * i + a if two else i
                    src = acc if name in ("C_out", "down21") else res
                    act.wait_ge(ss_added, t + 8 * EVENT[name] - (3 if two else 1))
                    nc.scalar.activation(work[:, (2 * par + a if two else par):(2 * par + a if two else par) + 1, :],
                                         src[:, bass.ds(t, 1), :], ACT.Square).then_inc(tile_sq, 1)

            def epilogue(name, b, i, par):
                s = st[name]
                ps = psum[:, 2 * par:2 * par + 2, :]
                act.wait_ge(mm_done, b + 1)
                if s.kind == "tokens":
                    dst = {"A_v": va, "B_v": bv, "C_va": cva, "C_vb": cvb}[name]
                    nc.scalar.copy(dst[:, :, bass.ds(i * 256, 256)],
                                   ps.rearrange("p a (t n) -> p (a t) n", n=256)).then_inc(block_out, 1)
                elif s.kind == "copy":
                    dst = {"A_qk": qk, "B_k": bk, "B_q": bq, "C_qka": qk, "C_qkb": qkb}[name]
                    nc.scalar.copy(dst[:, bass.ds(i * 2, 2), :], ps).then_inc(block_out, 1)
                elif s.kind == "sigmoid":
                    nc.scalar.activation(og[:, bass.ds(i * 2, 2), :], ps, ACT.Sigmoid).then_inc(block_out, 1)
                elif s.kind == "up":
                    nc.scalar.activation(work[:, 0, :], ps[:, 0, :], ACT.Sigmoid).then_inc(h_sig, 1)
                    act.wait_ge(block_out, b + 1)
                    nc.scalar.copy(hidh[:, bass.ds(i, 1), :], work[:, 2 + par:3 + par, :]).then_inc(h_hi, 1)
                elif s.kind in ("residual", "store", "down"):
                    if s.squares:
                        squares(name, b, i, par)

            def merge_epilogue(s, b, j, par):
                act.wait_ge(mm_done, b + 1)
                if par == 0:
                    nc.scalar.activation(work[:, 0, :], psum[:, 0, :], ACT.Sigmoid,
                                         bias=gains[:, bass.ds(j + BGATE2, 1)])
                    nc.scalar.activation(work[:, 1, :], psum[:, 1, :], ACT.Sigmoid,
                                         bias=gains[:, bass.ds(j + BGATE2 + DT, 1)]).then_inc(block_out, 1)
                else:
                    act.wait_ge(m_sum, s.m0 + j + 1)
                    nc.scalar.copy(mgh[:, bass.ds(j, 1), :], work[:, 2:3, :]).then_inc(m_hi, 1)

            def linear(name):
                s = st[name]

                def step(j, par):
                    b = s.b0 + 2 * j + par
                    split(s.b0 // 2 + j + par, b + 1, 1 - par, weights_of(s, 1 - par))
                    finish(j, par)

                def finish(j, par):
                    b = s.b0 + 2 * j + par
                    if s.kind == "merge":
                        merge_epilogue(s, b, j, par)
                    else:
                        epilogue(name, b, 2 * j + par, par)

                run_pairs(nc.scalar, s, step)
                last = s.blocks // 2 - 1
                step(last, 0)
                if s.next:
                    split(s.next.b0 // 2, s.next.b0, 0, weights_of(s.next, 0))
                finish(last, 1)

            def root(k):
                act.wait_ge(norm_sum, k + 1)
                nc.scalar.activation(rs[:, :], psum[:, 4, :], ACT.Sqrt, bias=eps[:, 0:1]).then_inc(norm_root, 1)

            def norm_split(n, used):
                if used:
                    act.wait_ge(mm_done, used)
                for t in range(DT):
                    act.wait_ge(n_full, DT * n + t + 1)
                    nc.scalar.copy(xh[:, t, :], work[:, t % 4, :]).then_inc(n_hi, 1)

            def feed_forward(f):
                nc.scalar.preload_act_table(ACT.Sigmoid)
                for half in range(2):
                    linear(f"up{f}{half}")
                    linear(f"down{f}{half}")

            def plain_squares(name, src):
                for t in range(DT):
                    act.wait_ge(sq_src, DT * {"final": 0, "post_mix": 1}[name] + t + 1)
                    act.wait_ge(ss_added, 8 * EVENT[name] + t - 3)
                    nc.scalar.activation(work[:, t % 4, :], src[:, t, :], ACT.Square).then_inc(tile_sq, 1)

            def softmax(which, yh):
                r = att[which]
                for t in range(r.units + r.lag + 4):
                    if t < r.units:
                        for m in range(r.maps):
                            g = r.s0 + t * r.maps + m
                            row = work[:, g % 4, 0:r.keys(t % TT)]
                            act.wait_ge(s_biased, g + 1)
                            nc.scalar.activation(row, row, ACT.Exp, bias=rowmax[:, g:g + 1], scale=-1.0,
                                                 accum_out=rowsum[:, g:g + 1]).then_inc(s_exp, 1)
                    u = t - r.lag
                    if 0 <= u < r.units:
                        h, qt = divmod(u, TT)
                        n = r.keys(qt) // P
                        act.wait_ge(t_done, r.u0 + u + 1)
                        if h >= 2:
                            act.wait_ge(pv_done, r.p0 + h - 1)
                        nc.scalar.copy(pt[:, h % 2, 0:n, qt * P:(qt + 1) * P],
                                       psum[:, 6 + (r.u0 + u) % 2, 0:n * P].rearrange("p (k q) -> p k q", q=P)
                                       ).then_inc(t_out, 1)
                    u = t - r.lag - 2
                    if 0 <= u < r.units and u % TT == TT - 1 and (u // TT + 1) % r.per_tile == 0:
                        y = r.y0 + (u // TT) // r.per_tile
                        act.wait_ge(pv_done, r.p0 + u // TT + 1)
                        if which == "DA":
                            nc.scalar.activation(datmp[:, 0, :], psum[:, y % 2, :], ACT.Square).then_inc(d_sq, 1)
                        else:
                            nc.scalar.copy(yh[:, y - r.y0, :], psum[:, y % 2, :]).then_inc(y_hi, 1)
                    u = t - r.lag - 3
                    if which == "DA" and 0 <= u < r.units and u % TT == TT - 1:
                        act.wait_ge(d_ss, u // TT + 1)
                        nc.scalar.activation(datmp[:, 0, :], psum[:, 2 + (r.y0 + u // TT) % 2, :], ACT.Ln,
                                             bias=eps[:, 1:2]).then_inc(d_ln, 1)
                        act.wait_ge(d_ln, u // TT + 1)
                        nc.scalar.activation(datmp[:, 0, :], datmp[:, 0, :], ACT.Exp, scale=-0.5).then_inc(d_rs, 1)
                        act.wait_ge(d_full, u // TT + 1)
                        nc.scalar.copy(yh[:, u // TT, :], datmp[:, 1, :]).then_inc(y_hi, 1)

            act.wait_ge(gain_t, 1)
            nc.scalar.copy(gains[:, :], psum[:, 7, 0:NGAIN]).then_inc(gain_out, 1)
            act.wait_ge(gate_in, 16)
            nc.scalar.copy(wgh[:, :, :], wg[:, :, :]).then_inc(wg_hi, 1)
            act.wait_ge(lam_step, 2)
            nc.scalar.activation(lam[0:1, 2:4], lam[0:1, 0:2], ACT.Exp).then_inc(lam_exp, 1)
            for t in range(DT):
                act.wait_ge(xt_done, t + 1)
                nc.scalar.copy(res[:, t, :], psum[:, 4 + t % 2, :]).then_inc(xt_out, 1)
                act.wait_ge(xt_out, t + 1)
                if t >= 4:
                    act.wait_ge(ss_added, t - 3)
                nc.scalar.activation(work[:, t % 4, :], res[:, t, :], ACT.Square).then_inc(tile_sq, 1)
            split(0, 0, 0, SLOT)
            act.wait_ge(const, 6)
            root(0)
            nc.scalar.preload_act_table_set(LN_EXP)
            norm_split(0, 0)
            act.wait_ge(g_step, 1)
            act.dma_start(gf[:, :], gi[A_HEADS:2 * A_HEADS, :]).then_inc(gf_in, 16)
            act.wait_ge(g_step, 2)
            nc.scalar.activation(lf[:, :], lf[:, :], ACT.Exp, scale=-1.0).then_inc(g_act, 1)
            act.wait_ge(g_act, 1)
            nc.scalar.activation(lf[:, :], lf[:, :], ACT.Ln, bias=1.0).then_inc(g_act, 1)
            nc.scalar.preload_act_table(ACT.Sigmoid)
            linear("A_qk")
            act.wait_ge(u_t, 1)
            nc.scalar.copy(ut[:, :, :], psum[:, 6, 0:TT * A_HEADS].rearrange("p (t h) -> p t h", t=TT)).then_inc(u_ready, 1)
            linear("A_v")
            linear("A_o")
            act.wait_ge(u_ready, 1)
            nc.scalar.preload_act_table_set(LN_EXP)
            for h in range(A_HEADS + 2):
                if h < A_HEADS:
                    act.wait_ge(a_mrow, h + 1)
                    if h >= 2:
                        act.wait_ge(a_step, 4 * (h - 2) + 1)
                    nc.scalar.activation(efl[:, h % 2, :], psum[:, 7, :], ACT.Exp).then_inc(a_floor, 1)
                    for t in range(TT):
                        if h >= 1:
                            act.wait_ge(a_p, TT * (h - 1) + t + 1)
                        nc.scalar.activation(work[:, t, 0:S - t * P], psum[:, 6, t * P:S], ACT.Exp,
                                             bias=ut[:, t, h:h + 1], scale=-1.0).then_inc(a_d, 1)
                if h >= 2:
                    act.wait_ge(a_ss, h - 1)
                    nc.scalar.activation(hr[:, :], psum[:, 2 + h % 2, :], ACT.Ln, bias=eps[:, 1:2]).then_inc(a_ln, 1)
                    act.wait_ge(a_ln, h - 1)
                    nc.scalar.activation(hr[:, :], hr[:, :], ACT.Exp, scale=-0.5).then_inc(a_rs, 1)
                    act.wait_ge(a_gated, h - 1)
                    nc.scalar.copy(xh[:, h - 2, :], og[:, h - 2, :]).then_inc(a_hi, 1)
                if 1 <= h <= A_HEADS:
                    act.wait_ge(a_den, h)
                    nc.scalar.activation(dn[:, :], psum[:, 2 + (h - 1) % 2, :], ACT.Abs).then_inc(a_abs, 1)
                    act.wait_ge(a_step, 4 * (h - 1) + 3)
                    if h >= 2:
                        act.wait_ge(a_ss, h - 1)
                    nc.scalar.activation(hq[:, :], hs[:, :], ACT.Square).then_inc(a_sq, 1)
            linear("A_out")
            root(1)
            norm_split(1, st["A_out"].b0 + 4)
            feed_forward(0)
            root(2)
            norm_split(2, st["down01"].b0 + 8)
            linear("B_k")
            linear("B_v")
            norm_split(3, st["B_v"].b0 + 4)
            linear("B_q")
            nc.scalar.preload_act_table(ACT.Exp)
            softmax("B", xh)
            linear("B_out")
            root(3)
            norm_split(4, st["B_out"].b0 + 4)
            feed_forward(1)
            root(4)
            plain_squares("final", res)
            root(5)
            norm_split(5, st["down11"].b0 + 8)
            for name in ("C_qka", "C_va", "C_qkb", "C_vb"):
                linear(name)
            nc.scalar.preload_act_table_set(LN_EXP)
            softmax("DA", yah)
            softmax("NA", ybh)
            nc.scalar.preload_act_table(ACT.Sigmoid)
            linear("C_merge")
            linear("C_out")
            root(6)
            plain_squares("post_mix", res)
            root(7)
            norm_split(6, st["C_out"].b0 + 4)
            feed_forward(2)
            root(8)
            for t in range(2 * TT):
                act.wait_ge(ot_done, t + 1)
                nc.scalar.copy(acc[:, t, :], psum[:, 4 + t % 2, :]).then_inc(ot_out, 1)

        @block.vector
        def _(dve):
            vec = nc.vector

            def split(b, par, n):
                dve.wait_ge(w_hi, b + 1)
                vec.tensor_tensor(wl[:, par, 0:n], stage[:, par, 0:n], wh[:, par, 0:n].bitcast(F32),
                                  ALU.subtract).then_inc(w_lo, 1)

            def add_square(event, t, buf):
                dve.wait_ge(tile_sq, t + 8 * event + 1)
                dve.wait_ge(ss_zero, event + 1)
                if not isinstance(t, int) or 8 * event + t:
                    dve.wait_ge(ss_added, t + 8 * event)
                vec.tensor_tensor(ss[:, :], ss[:, :], work[:, buf, :], ALU.add).then_inc(ss_added, 1)

            def epilogue(name, b, i, par):
                s = st[name]
                ps = psum[:, 2 * par:2 * par + 2, :]
                if s.kind == "up":
                    t = s.h0 + i
                    dve.wait_ge(h_sig, t + 1)
                    vec.tensor_tensor(work[:, 1, :], work[:, 0, :], ps[:, 0, :], ALU.mult).then_inc(h_act, 1)
                    dve.wait_ge(h_act, t + 1)
                    vec.tensor_tensor(work[:, 2 + par, :], work[:, 1, :], ps[:, 1, :], ALU.mult).then_inc(block_out, 1)
                    dve.wait_ge(h_hi, t + 1)
                    vec.tensor_tensor(hidl[:, bass.ds(i, 1), :], work[:, 2 + par:3 + par, :],
                                      hidh[:, bass.ds(i, 1), :].bitcast(F32), ALU.subtract).then_inc(h_lo, 1)
                elif s.kind == "residual":
                    dve.wait_ge(mm_done, b + 1)
                    r = res[:, bass.ds(2 * i, 2), :]
                    vec.tensor_tensor(r, r, ps, ALU.add).then_inc(block_out, 1)
                    for a in range(2):
                        add_square(EVENT[name], 2 * i + a, 2 * par + a)
                elif s.kind == "store":
                    dve.wait_ge(mm_done, b + 1)
                    vec.tensor_copy(acc[:, bass.ds(2 * i, 2), :], ps).then_inc(block_out, 1)
                    for a in range(2):
                        add_square(EVENT[name], 2 * i + a, 2 * par + a)
                elif s.kind == "down":
                    f, half = int(name[4]), int(name[5])
                    dve.wait_ge(mm_done, b + 1)
                    r = (acc if f == 2 else res)[:, bass.ds(i, 1), :]
                    if half == 1:
                        dve.wait_ge(block_out, st[f"down{f}0"].b0 + 8)
                    if f == 2 and half == 0:
                        vec.tensor_copy(r, ps[:, 0:1, :]).then_inc(block_out, 1)
                    else:
                        vec.tensor_tensor(r, r, ps[:, 0:1, :], ALU.add).then_inc(block_out, 1)
                    if half == 1:
                        add_square(EVENT[name], i, par)

            def merge_epilogue(s, b, j, par):
                if par == 0:
                    return
                dve.wait_ge(block_out, b)
                dve.wait_ge(mm_done, b + 1)
                vec.tensor_tensor(work[:, 0, :], work[:, 0, :], psum[:, 2, :], ALU.mult).then_inc(m_a, 1)
                vec.tensor_tensor(work[:, 1, :], work[:, 1, :], psum[:, 3, :], ALU.mult).then_inc(block_out, 1)
                dve.wait_ge(m_a, s.m0 + j + 1)
                dve.wait_ge(block_out, b + 1)
                vec.tensor_tensor(work[:, 2, :], work[:, 0, :], work[:, 1, :], ALU.add).then_inc(m_sum, 1)
                dve.wait_ge(m_hi, s.m0 + j + 1)
                vec.tensor_tensor(mgl[:, bass.ds(j, 1), :], work[:, 2:3, :],
                                  mgh[:, bass.ds(j, 1), :].bitcast(F32), ALU.subtract).then_inc(m_lo, 1)

            def linear(name):
                s = st[name]

                def step(j, par):
                    split(s.b0 + 2 * j + par + 1, 1 - par, weights_of(s, 1 - par))
                    finish(j, par)

                def finish(j, par):
                    b = s.b0 + 2 * j + par
                    if s.kind == "merge":
                        merge_epilogue(s, b, j, par)
                    else:
                        epilogue(name, b, 2 * j + par, par)

                run_pairs(vec, s, step)
                last = s.blocks // 2 - 1
                step(last, 0)
                if s.next:
                    split(s.next.b0, 0, weights_of(s.next, 0))
                finish(last, 1)

            def norm_scale(k):
                dve.wait_ge(norm_root, k + 1)
                vec.reciprocal(rs[:, :], rs[:, :]).then_inc(norm_rs, 1)
                vec.memset(ss[:, :], 0.0).then_inc(ss_zero, 1)
                dve.wait_ge(norm_rs, k + 1)

            def norm(n, gain):
                for t in range(DT + 1):
                    if t < DT:
                        vec.scalar_tensor_tensor(out=work[:, t % 4, :], in0=res[:, t, :],
                                                 scalar=gains[:, gain + t:gain + t + 1], in1=rs[:, :],
                                                 op0=ALU.mult, op1=ALU.mult).then_inc(n_full, 1)
                    if t >= 1:
                        dve.wait_ge(n_hi, DT * n + t)
                        vec.tensor_tensor(xl[:, t - 1, :], work[:, (t - 1) % 4, :],
                                          xh[:, t - 1, :].bitcast(F32), ALU.subtract).then_inc(n_lo, 1)

            def feed_forward(f):
                for half in range(2):
                    linear(f"up{f}{half}")
                    linear(f"down{f}{half}")

            def softmax(which, yh, yl):
                r = att[which]
                for t in range(r.units + r.lag + 5):
                    if t < r.units:
                        h, qt = divmod(t, TT)
                        n = r.keys(qt)
                        for m in range(r.maps):
                            g = r.s0 + t * r.maps + m
                            row = work[:, g % 4, 0:n]
                            scores = psum[:, 4 + g % 2, 0:n]
                            if which == "B":
                                bias = relt[:, h, n - 1::-1] if n == S else relt[:, h, 0:n][:, ::-1]
                            elif which == "DA":
                                bias = absd[:, 384 - qt * P:384 - qt * P + S]
                                dve.wait_ge(absd_scaled, h + 1)
                            else:
                                ro = 6 - 2 * qt
                                bias = rpt[:, h % 2, ro:ro + 8, ::-1]
                                row = row.rearrange("p (a b) -> p a b", b=GRID_W)
                                scores = scores.rearrange("p (a b) -> p a b", b=GRID_W)
                                dve.wait_ge(rpt_ready, h + 1)
                            dve.wait_ge(s_done, g + 1)
                            back = t * r.maps + m - 4
                            dve.wait_ge(t_done, r.u0 + (back // r.maps + 1 if back >= 0 else 0))
                            vec.tensor_tensor_reduce(row, scores, bias, -SCALE, 3e38, ALU.add, ALU.min,
                                                     rowmax[:, g:g + 1]).then_inc(s_biased, 1)
                        if which == "DA" and qt == TT - 1 and h < r.heads - 1:
                            dve.wait_ge(s_biased, r.s0 + (t + 1) * r.maps)
                            vec.tensor_scalar(absd[:, :], absd[:, :], 0.25, None, ALU.mult).then_inc(absd_scaled, 1)
                    u = t - 1
                    if 0 <= u < r.units:
                        g = r.s0 + u * r.maps
                        n = r.keys(u % TT)
                        dve.wait_ge(s_exp, g + r.maps)
                        vec.reciprocal(rowinv[:, g:g + r.maps], rowsum[:, g:g + r.maps]).then_inc(s_inv, 1)
                        row = work[:, g % 4, 0:n]
                        if r.maps == 1:
                            dve.wait_ge(s_inv, r.i0 + u + 1)
                            vec.tensor_scalar(row, row, rowinv[:, g:g + 1], None, ALU.mult).then_inc(s_prob, 1)
                        else:
                            dve.wait_ge(s_inv, r.i0 + 3 * u + 1)
                            vec.tensor_scalar(rowinv[:, g + 1:g + 2], rowinv[:, g + 1:g + 2], lam[:, 5:6], None,
                                              ALU.mult).then_inc(s_inv, 1)
                            vec.tensor_scalar(row, row, rowinv[:, g:g + 1], None, ALU.mult).then_inc(s_inv, 1)
                            dve.wait_ge(s_inv, r.i0 + 3 * u + 3)
                            vec.scalar_tensor_tensor(out=row, in0=work[:, (g + 1) % 4, 0:n],
                                                     scalar=rowinv[:, g + 1:g + 2], in1=row,
                                                     op0=ALU.mult, op1=ALU.add).then_inc(s_prob, 1)
                    u = t - r.lag - 3
                    if 0 <= u < r.units and u % TT == TT - 1 and (u // TT + 1) % r.per_tile == 0:
                        y = r.y0 + (u // TT) // r.per_tile
                        if which == "DA":
                            h = u // TT
                            dve.wait_ge(d_rs, h + 1)
                            vec.scalar_tensor_tensor(out=datmp[:, 1, :], in0=psum[:, y % 2, :],
                                                     scalar=gains[:, SUBLN:SUBLN + 1], in1=datmp[:, 0, :],
                                                     op0=ALU.mult, op1=ALU.mult).then_inc(d_full, 1)
                            dve.wait_ge(y_hi, y + 1)
                            vec.tensor_tensor(yl[:, h, :], datmp[:, 1, :], yh[:, h, :].bitcast(F32),
                                              ALU.subtract).then_inc(y_lo, 1)
                        else:
                            dve.wait_ge(y_hi, y + 1)
                            vec.tensor_tensor(yl[:, y - r.y0, :], psum[:, y % 2, :], yh[:, y - r.y0, :].bitcast(F32),
                                              ALU.subtract).then_inc(y_lo, 1)

            vec.memset(ss[:, :], 0.0).then_inc(ss_zero, 1)
            dve.wait_ge(tab_in, 32)
            first = MAX_REL - (P - 1)
            vec.tensor_scalar(ext[:, 0:N_REL - first], extsrc[:, first:N_REL], UP, None, ALU.mult).then_inc(tab_step, 1)
            dve.wait_ge(tab_step, 1)
            vec.tensor_copy(ext[:, N_REL - first:EXT],
                            ext[:, N_REL - first - 1:N_REL - first].to_broadcast([B_HEADS, EXT - N_REL + first])
                            ).then_inc(tab_step, 1)
            dve.wait_ge(const, 6)
            vec.tensor_scalar(rppad[:, 48:79], rpsrc[:, ::-1], UP, None, ALU.mult).then_inc(tab_step, 1)
            dve.wait_ge(gain_out, 1)
            vec.tensor_scalar(gains[:, 0:GHEAD], gains[:, 0:GHEAD], math.sqrt(D), None, ALU.mult).then_inc(gain_ready, 1)
            vec.tensor_scalar(gains[:, GHEAD:BGATE2], gains[:, GHEAD:BGATE2], math.sqrt(A_DV), None,
                              ALU.mult).then_inc(gain_ready, 1)
            vec.tensor_scalar(gains[:, SUBLN:NGAIN], gains[:, SUBLN:NGAIN], (1.0 - LAMBDA_INIT) * math.sqrt(2 * DH),
                              None, ALU.mult).then_inc(gain_ready, 1)
            dve.wait_ge(wg_hi, 1)
            vec.tensor_tensor(wgl[:, :, :], wg[:, :, :], wgh[:, :, :].bitcast(F32), ALU.subtract).then_inc(wg_lo, 1)
            for i in range(2):
                vec.tensor_tensor_reduce(lrow[0:1, 2 * i, :], lrow[0:1, 2 * i, :], lrow[0:1, 2 * i + 1, :], 1.0, 0.0,
                                         ALU.mult, ALU.add, lam[0:1, i:i + 1]).then_inc(lam_step, 1)
            dve.wait_ge(lam_exp, 1)
            vec.tensor_tensor(lam[0:1, 4:5], lam[0:1, 3:4], lam[0:1, 2:3], ALU.subtract).then_inc(lam_step, 1)
            dve.wait_ge(lam_step, 3)
            vec.tensor_scalar(lam[0:1, 4:5], lam[0:1, 4:5], -LAMBDA_INIT, None, ALU.add).then_inc(lam_step, 1)
            dve.wait_ge(lam_mm, 1)
            vec.tensor_copy(lam[:, 5:6], psum[:, 7, 256:257]).then_inc(lam_step, 1)
            for t in range(DT):
                add_square(0, t, t % 4)
            split(0, 0, SLOT)
            norm_scale(0)
            dve.wait_ge(gain_ready, 3)
            norm(0, MIX0)
            dve.wait_ge(g_done, 1)
            vec.tensor_scalar(gi[:, :], psum[0:16, 5, :], brow[:, 0:1], None, ALU.add).then_inc(g_step, 1)
            dve.wait_ge(gf_in, 16)
            vec.scalar_tensor_tensor(out=lf[:, :], in0=gf[:, :], scalar=-1.0, in1=gf[:, :],
                                     op0=ALU.mult, op1=ALU.max).then_inc(g_step, 1)
            vec.tensor_scalar(gf[:, :], gf[:, :], 0.0, None, ALU.min).then_inc(g_step, 1)
            dve.wait_ge(g_act, 2)
            dve.wait_ge(g_step, 3)
            vec.tensor_tensor(lf[:, :], gf[:, :], lf[:, :], ALU.subtract).then_inc(g_step, 1)
            dve.wait_ge(g_step, 4)
            vec.tensor_tensor_scan(gb[:, :], ones[0:A_HEADS, 0:1].to_broadcast([A_HEADS, S]), lf[:, :], 0.0,
                                   ALU.mult, ALU.add).then_inc(g_step, 1)
            dve.wait_ge(g_step, 5)
            vec.tensor_tensor(gu[:, :], gi[0:A_HEADS, :], gb[:, :], ALU.subtract).then_inc(g_step, 1)
            dve.wait_ge(g_step, 6)
            vec.tensor_tensor_scan(gm[:, :], gu[:, :], gu[:, :], NEG, ALU.max, ALU.max).then_inc(g_step, 1)
            dve.wait_ge(g_step, 7)
            vec.scalar_tensor_tensor(out=gn[:, :], in0=gb[:, :], scalar=-1.0, in1=gm[:, :],
                                     op0=ALU.mult, op1=ALU.subtract).then_inc(g_step, 1)
            for name in ("A_qk", "A_v", "A_o"):
                linear(name)
            dve.wait_ge(block_out, st["A_o"].b0 + 4)
            for h in range(A_HEADS + 2):
                if h < A_HEADS:
                    for t in range(TT):
                        g = TT * h + t
                        dve.wait_ge(a_s, g + 1)
                        dve.wait_ge(a_mask, g + 1)
                        if h >= 2:
                            dve.wait_ge(a_den, h - 1)
                        n = S - t * P
                        vec.scalar_tensor_tensor(out=pt[:, h % 2, t, 0:n], in0=psum[:, 4 + g % 2, 0:n], scalar=SCALE,
                                                 in1=work[:, t, 0:n], op0=ALU.mult, op1=ALU.mult).then_inc(a_p, 1)
                if h >= 2:
                    e = h - 2
                    dve.wait_ge(a_rs, e + 1)
                    dve.wait_ge(a_step, 4 * e + 3)
                    vec.scalar_tensor_tensor(out=hn[:, :], in0=hs[:, :], scalar=gains[:, GHEAD + e:GHEAD + e + 1],
                                             in1=hr[:, :], op0=ALU.mult, op1=ALU.mult).then_inc(a_step, 1)
                    dve.wait_ge(a_step, 4 * e + 4)
                    vec.tensor_tensor(og[:, e, :], og[:, e, :], hn[:, :], ALU.mult).then_inc(a_gated, 1)
                if 1 <= h <= A_HEADS:
                    e = h - 1
                    dve.wait_ge(a_abs, e + 1)
                    vec.tensor_tensor(dn[:, :], dn[:, :], efl[:, e % 2, :], ALU.max).then_inc(a_step, 1)
                    dve.wait_ge(a_step, 4 * e + 1)
                    vec.reciprocal(dn[:, :], dn[:, :]).then_inc(a_step, 1)
                    dve.wait_ge(a_step, 4 * e + 2)
                    vec.tensor_tensor(hs[:, :], psum[:, e % 2, :], dn[:, :], ALU.mult).then_inc(a_step, 1)
                if h >= 2:
                    e = h - 2
                    dve.wait_ge(a_hi, e + 1)
                    vec.tensor_tensor(xl[:, e, :], og[:, e, :], xh[:, e, :].bitcast(F32), ALU.subtract).then_inc(a_lo, 1)
            linear("A_out")
            norm_scale(1)
            norm(1, FFN0)
            feed_forward(0)
            norm_scale(2)
            norm(2, KVN)
            linear("B_k")
            linear("B_v")
            norm(3, MIX1)
            linear("B_q")
            dve.wait_ge(relt_ready, 1)
            softmax("B", xh, xl)
            linear("B_out")
            norm_scale(3)
            norm(4, FFN1)
            feed_forward(1)
            norm_scale(4)
            for t in range(DT + 1):
                if t < DT:
                    vec.scalar_tensor_tensor(out=res[:, t, :], in0=res[:, t, :], scalar=gains[:, FINAL + t:FINAL + t + 1],
                                             in1=rs[:, :], op0=ALU.mult, op1=ALU.mult).then_inc(sq_src, 1)
                if t >= 1:
                    add_square(5, t - 1, (t - 1) % 4)
            norm_scale(5)
            norm(5, PREMIX)
            for name in ("C_qka", "C_va", "C_qkb", "C_vb"):
                linear(name)
            dve.wait_ge(absd_ready, 1)
            vec.scalar_tensor_tensor(out=absd[:, :], in0=absd[:, :], scalar=-1.0, in1=absd[:, :],
                                     op0=ALU.mult, op1=ALU.min).then_inc(absd_scaled, 1)
            softmax("DA", yah, yal)
            softmax("NA", ybh, ybl)
            linear("C_merge")
            linear("C_out")
            norm_scale(6)
            for t in range(DT):
                vec.scalar_tensor_tensor(out=acc[:, t, :], in0=acc[:, t, :], scalar=gains[:, POSTMIX + t:POSTMIX + t + 1],
                                         in1=rs[:, :], op0=ALU.mult, op1=ALU.mult).then_inc(post_scaled, 1)
            for t in range(DT + 1):
                if t < DT:
                    dve.wait_ge(post_scaled, t + 1)
                    vec.tensor_tensor(res[:, t, :], res[:, t, :], acc[:, t, :], ALU.add).then_inc(sq_src, 1)
                if t >= 1:
                    add_square(7, t - 1, (t - 1) % 4)
            norm_scale(7)
            norm(6, PREFFN)
            feed_forward(2)
            norm_scale(8)
            for t in range(DT):
                vec.scalar_tensor_tensor(out=acc[:, t, :], in0=acc[:, t, :], scalar=gains[:, POSTFFN + t:POSTFFN + t + 1],
                                         in1=rs[:, :], op0=ALU.mult, op1=ALU.mult).then_inc(post_scaled, 1)
            for t in range(DT):
                dve.wait_ge(post_scaled, DT + t + 1)
                vec.tensor_tensor(res[:, t, :], res[:, t, :], acc[:, t, :], ALU.add).then_inc(sq_src, 1)

        @block.tensor
        def _(pe):
            mm = nc.tensor.matmul

            def three(out, a_hi, a_lo, b_hi, b_lo, start, stop):
                mm(out, a_hi, b_lo, start=start, stop=False)
                mm(out, a_lo, b_hi, start=False, stop=False)
                return mm(out, a_hi, b_hi, start=False, stop=stop)

            def ready(name):
                if name in ("A_qk", "A_v", "A_o"):
                    return n_lo, 0
                if name == "A_out":
                    return a_lo, 0
                if name[:2] == "up":
                    return n_lo, DT * {"0": 1, "1": 4, "2": 6}[name[2]]
                if name[:4] == "down":
                    return h_lo, st["up" + name[4:]].h0
                return {"B_k": (n_lo, DT * 2), "B_v": (n_lo, DT * 2), "B_q": (n_lo, DT * 3),
                        "B_out": (y_lo, att["B"].y0), "C_out": (m_lo, 0)}.get(name, (n_lo, DT * 5))

            def multiply(name, b, par, first):
                s = st[name]
                pe.wait_ge(w_lo, b + 1)
                if not isinstance(b, int) or b >= 2:
                    pe.wait_ge(block_out, b - 1)
                sem_, count = ready(name)
                inh, inl = {"down": (hidh, hidl), "store": (mgh, mgl)}.get(s.kind, (xh, xl))
                kt = s.kt
                whp, wlp = wh[:, par], wl[:, par]
                if s.kind == "tokens":
                    for t in range(TT):
                        o = psum[:, 2 * par + t // 2, 256 * (t % 2):256 * (t % 2) + 256]
                        for k in range(kt):
                            if first and t == 0:
                                pe.wait_ge(sem_, count + k + 1)
                            last = three(o, inh[:, k, t * P:(t + 1) * P], inl[:, k, t * P:(t + 1) * P],
                                         whp[:, k * 256:(k + 1) * 256], wlp[:, k * 256:(k + 1) * 256],
                                         k == 0, k == kt - 1)
                elif s.kind == "up":
                    for a in range(2):
                        for k in range(DT):
                            if first and a == 0:
                                pe.wait_ge(sem_, count + k + 1)
                            c = (a * DT + k) * P
                            last = three(psum[:, 2 * par + a, :], whp[:, c:c + P], wlp[:, c:c + P],
                                         inh[:, k, :], inl[:, k, :], k == 0, k == DT - 1)
                elif s.kind == "down":
                    for k in range(kt):
                        if first:
                            pe.wait_ge(sem_, count + k + 1)
                        last = three(psum[:, 2 * par, :], whp[:, k * P:(k + 1) * P], wlp[:, k * P:(k + 1) * P],
                                     inh[:, k, :], inl[:, k, :], k == 0, k == kt - 1)
                else:
                    for a in range(2):
                        for k in range(kt):
                            if first and a == 0:
                                pe.wait_ge(sem_, count + k + 1)
                            c = k * 256 + a * P
                            last = three(psum[:, 2 * par + a, :], whp[:, c:c + P], wlp[:, c:c + P],
                                         inh[:, k, :], inl[:, k, :], k == 0, k == kt - 1)
                last.then_inc(mm_done, 1)

            def merge(b, par):
                pe.wait_ge(w_lo, b + 1)
                pe.wait_ge(block_out, b - 1)
                kt = DT if par == 0 else 4
                for a in range(2):
                    inh, inl = (xh, xl) if par == 0 else ((yah, yal), (ybh, ybl))[a]
                    for k in range(kt):
                        c = (a * kt + k) * P
                        last = three(psum[:, 2 * par + a, :], wh[:, par, c:c + P], wl[:, par, c:c + P],
                                     inh[:, k, :], inl[:, k, :], k == 0, k == kt - 1)
                last.then_inc(mm_done, 1)

            def linear(name):
                s = st[name]
                if s.kind == "merge":
                    pe.wait_ge(y_lo, att["NA"].y0 + 4)
                    with nc.tensor.Fori(0, s.blocks // 2) as j:
                        merge(s.b0 + 2 * j, 0)
                        merge(s.b0 + 2 * j + 1, 1)
                    return
                multiply(name, s.b0, 0, True)
                multiply(name, s.b0 + 1, 1, False)
                if s.blocks == 4:
                    multiply(name, s.b0 + 2, 0, False)
                    multiply(name, s.b0 + 3, 1, False)
                elif s.blocks > 4:
                    with nc.tensor.Fori(1, s.blocks // 2) as j:
                        multiply(name, s.b0 + 2 * j, 0, False)
                        multiply(name, s.b0 + 2 * j + 1, 1, False)

            def norm_total(k):
                pe.wait_ge(ss_added, 8 * (k + 1))
                mm(psum[:, 4, :], ones[:, :], ss[:, :], start=True, stop=True).then_inc(norm_sum, 1)

            def feed_forward(f):
                for half in range(2):
                    linear(f"up{f}{half}")
                    linear(f"down{f}{half}")

            def softmax(which, q_of, k_of, v_of):
                r = att[which]
                for t in range(r.units + r.lag + 4):
                    if t < r.units:
                        h, qt = divmod(t, TT)
                        for m in range(r.maps):
                            g = r.s0 + t * r.maps + m
                            if g >= 2:
                                pe.wait_ge(s_biased, g - 1)
                            mm(psum[:, 4 + g % 2, 0:r.keys(qt)], q_of(h, m)[:, qt * P:(qt + 1) * P],
                               k_of(h, m)[:, 0:r.keys(qt)], start=True, stop=True).then_inc(s_done, 1)
                    u = t - r.lag
                    if 0 <= u < r.units:
                        g = r.s0 + u * r.maps
                        n = r.keys(u % TT) // P
                        pe.wait_ge(s_prob, r.u0 + u + 1)
                        if r.u0 + u >= 2:
                            pe.wait_ge(t_out, r.u0 + u - 1)
                        for k in range(n):
                            last = nc.tensor.transpose(psum[:, 6 + (r.u0 + u) % 2, k * P:(k + 1) * P],
                                                       work[:, g % 4, k * P:(k + 1) * P], ident[:, :])
                        last.then_inc(t_done, 1)
                    u = t - r.lag - 1
                    if 0 <= u < r.units and u % TT == TT - 1:
                        h = u // TT
                        y = r.y0 + h // r.per_tile
                        pe.wait_ge(t_out, r.u0 + u + 1)
                        if y >= 2:
                            pe.wait_ge(y_lo, y - 1)
                        width = P // r.per_tile
                        rows = width * (h % r.per_tile)
                        for k in range(TT):
                            q0 = k * P if r.causal else 0
                            last = mm(psum[rows:rows + width, y % 2, q0:S], v_of(h, k), pt[:, h % 2, k, q0:S],
                                      start=(k == 0), stop=(k == TT - 1))
                        last.then_inc(pv_done, 1)
                    u = t - r.lag - 2
                    if which == "DA" and 0 <= u < r.units and u % TT == TT - 1:
                        y = r.y0 + u // TT
                        pe.wait_ge(d_sq, u // TT + 1)
                        mm(psum[:, 2 + y % 2, :], ones[:, :], datmp[:, 0, :], start=True, stop=True).then_inc(d_ss, 1)

            pe.wait_ge(const, 8)
            pe.wait_ge(small_in, 16 * 18)
            nc.tensor.transpose(psum[:, 7, 0:NGAIN], gload[0:NGAIN, :], ident[0:NGAIN, 0:NGAIN]).then_inc(gain_t, 1)
            pe.wait_ge(lam_step, 4)
            pe.wait_ge(gain_out, 1)
            mm(psum[:, 7, 256:257], ones[0:1, :], lam[0:1, 4:5], start=True, stop=True).then_inc(lam_mm, 1)
            pe.wait_ge(x_in, 16 * TT)
            for k in range(DT):
                if k >= 2:
                    pe.wait_ge(xt_out, k - 1)
                for t in range(TT):
                    last = nc.tensor.transpose(psum[:, 4 + k % 2, t * P:(t + 1) * P], xin[:, t, k * P:(k + 1) * P],
                                               ident[:, :])
                last.then_inc(xt_done, 1)
            pe.wait_ge(xt_out, DT)
            norm_total(0)
            pe.wait_ge(wg_lo, 1)
            for k in range(DT):
                pe.wait_ge(n_lo, k + 1)
                last = three(psum[0:16, 5, :], wgh[:, k, :], wgl[:, k, :], xh[:, k, :], xl[:, k, :],
                             k == 0, k == DT - 1)
            last.then_inc(g_done, 1)
            linear("A_qk")
            pe.wait_ge(g_step, 8)
            for t in range(TT):
                last = nc.tensor.transpose(psum[:, 6, t * A_HEADS:(t + 1) * A_HEADS], gu[:, t * P:(t + 1) * P],
                                           ident[0:A_HEADS, 0:A_HEADS])
            last.then_inc(u_t, 1)
            linear("A_v")
            linear("A_o")
            pe.wait_ge(block_out, st["A_o"].b0 + 4)
            pe.wait_ge(u_ready, 1)
            for h in range(A_HEADS + 2):
                if h < A_HEADS:
                    if h >= 1:
                        pe.wait_ge(a_d, TT * h)
                    mm(psum[:, 6, :], sel[:, h, :], gm[:, :], start=True, stop=True)
                    if h >= 1:
                        pe.wait_ge(a_floor, h)
                    mm(psum[:, 7, :], sel[:, h, :], gn[:, :], start=True, stop=True).then_inc(a_mrow, 1)
                    rows = slice(A_DQK * (h % 2), A_DQK * (h % 2) + A_DQK)
                    for t in range(TT):
                        g = TT * h + t
                        if g >= 2:
                            pe.wait_ge(a_p, g - 1)
                        mm(psum[:, 4 + g % 2, 0:S - t * P], qk[rows, 4 + h // 2, t * P:(t + 1) * P],
                           qk[rows, h // 2, t * P:S], start=True, stop=True).then_inc(a_s, 1)
                if h >= 2:
                    pe.wait_ge(a_sq, h - 1)
                    mm(psum[:, 2 + (h - 2) % 2, :], ones[:, :], hq[:, :], start=True, stop=True).then_inc(a_ss, 1)
                if 1 <= h <= A_HEADS:
                    e = h - 1
                    pe.wait_ge(a_p, TT * (e + 1))
                    if e >= 2:
                        pe.wait_ge(a_rs, e - 1)
                    for t in range(TT):
                        mm(psum[:, e % 2, t * P:S], va[:, t, e * A_DV:(e + 1) * A_DV], pt[:, e % 2, t, 0:S - t * P],
                           start=(t == 0), stop=(t == TT - 1))
                    for t in range(TT):
                        last = mm(psum[:, 2 + e % 2, t * P:S], ones[:, :], pt[:, e % 2, t, 0:S - t * P],
                                  start=(t == 0), stop=(t == TT - 1))
                    last.then_inc(a_den, 1)
            linear("A_out")
            norm_total(1)
            feed_forward(0)
            norm_total(2)
            for name in ("B_k", "B_v", "B_q"):
                linear(name)
            pe.wait_ge(block_out, st["B_q"].b0 + 4)

            def half(tensor, h, tile0=0):
                return tensor[DH * (h % 2):DH * (h % 2) + DH, tile0 + h // 2, :]

            softmax("B", lambda h, m: half(bq, h), lambda h, m: half(bk, h),
                    lambda h, k: bv[:, k, h * DH:(h + 1) * DH])
            linear("B_out")
            norm_total(3)
            feed_forward(1)
            norm_total(4)
            norm_total(5)
            for name in ("C_qka", "C_va", "C_qkb", "C_vb"):
                linear(name)
            pe.wait_ge(block_out, st["C_vb"].b0 + 2)
            softmax("DA", lambda h, m: half(qk, 2 * h + m), lambda h, m: half(qk, 2 * h + m, 4),
                    lambda h, k: cva[:, k, h * P:(h + 1) * P])
            softmax("NA", lambda h, m: half(qkb, h), lambda h, m: half(qkb, h, 4),
                    lambda h, k: cvb[:, k, h * DH:(h + 1) * DH])
            linear("C_merge")
            linear("C_out")
            norm_total(6)
            norm_total(7)
            feed_forward(2)
            norm_total(8)
            pe.wait_ge(sq_src, 3 * DT)
            for i in range(2 * TT):
                t, a = divmod(i, 2)
                if i >= 2:
                    pe.wait_ge(ot_out, i - 1)
                for k in range(4):
                    last = nc.tensor.transpose(psum[:, 4 + i % 2, k * P:(k + 1) * P],
                                               res[:, 4 * a + k, t * P:(t + 1) * P], ident[:, :])
                last.then_inc(ot_done, 1)


_INS = ["x", "a_w_in", "a_b_gate", "a_g_head", "a_w_out", "b_w_q", "b_rel_bias", "b_w_o", "kv_norm_g", "w_kv",
        "norm_mix_g", "norm_ffn_g", "ffn_w_gate", "ffn_w_up", "ffn_w_down", "final_norm_g", "pre_mix_w_2", "w_in_2",
        "b_gate_2", "lambda_q1_2", "lambda_k1_2", "lambda_q2_2", "lambda_k2_2", "subln_w_2", "rpb_2",
        "w_branch_a_2", "w_branch_b_2", "w_out_2", "post_mix_w_2", "pre_ffn_w_2", "w_gate_2", "w_up_2", "w_down_2",
        "post_ffn_w_2"]


def kernel(**inputs):
    import concourse.bacc as _bacc
    import numpy as _np
    from concourse.bass_utils import run_bass_kernel_spmd as _run

    nc = _bacc.Bacc("TRN2", target_bir_lowering=False, num_devices=1)
    arrays, args = {}, []
    for name in _INS:
        a = _np.ascontiguousarray(inputs[name])
        arrays[f"in_{name}_dram"] = a
        args.append(nc.dram_tensor(f"in_{name}_dram", a.shape, mybir.dt.from_np(a.dtype), kind="ExternalInput").ap())
    args.append(nc.dram_tensor("out_dram", (1, S, D), F32, kind="ExternalOutput").ap())
    build(nc, *args)
    r = _run(nc, [arrays], core_ids=[0])
    return r.results[0]["out_dram"]
```

```python
import math
from contextlib import ExitStack

import concourse.bass as bass
from concourse import mybir

F32 = mybir.dt.float32
F32R = mybir.dt.float32r
ACT = mybir.ActivationFunctionType
ALU = mybir.AluOpType

P = 128
S = 512
D = 1024
DT = D // P
TT = S // P
EPS = 1e-6
CHUNK = 64
A_HEADS, A_DQK, A_DV = 8, 64, 128
B_HEADS, DH = 16, 64
MAX_REL = 256
N_REL = 2 * MAX_REL + 1
DFF = 2816
HALVES = (12, 10)
DA_HEADS = 4
NA_HEADS, NA_ROWS, NA_COLS, GRID_W = 8, 8, 16, 64
NEG = -1e30
LN_EXP = "natural_log_exp_and_others"
LAMBDA_INIT = 0.8 - 0.6 * math.exp(0.0)
SCALE = DH ** -0.5
UP = 1.0 / SCALE
SLOT = 8 * 256

(MIX0, FFN0, KVN, MIX1, FFN1, FINAL, PREMIX, POSTMIX, PREFFN, POSTFFN) = (8 * i for i in range(10))
GHEAD, BGATE2, SUBLN, NGAIN = 80, 88, 104, 105
FINPRE = NGAIN
EXT = 640
RPW = 127
NRO = 14


class Stage:

    def __init__(self, kind, blocks, kt=DT):
        self.kind, self.blocks, self.kt = kind, blocks, kt
        self.elems = {"merge": None, "down": kt * P}.get(kind, SLOT)


def plan():
    st = {}

    def add(name, kind, blocks, kt=DT, squares=False):
        st[name] = Stage(kind, blocks, kt)
        st[name].squares = squares

    add("A_qk", "copy", 4)
    add("A_v", "tokens", 4)
    add("A_o", "sigmoid", 4)
    add("A_out", "residual", 4, squares=True)
    for f in range(3):
        if f == 1:
            add("B_k", "copy", 4)
            add("B_v", "tokens", 4)
            add("B_q", "copy", 4)
            add("B_out", "residual", 4, squares=True)
        if f == 2:
            add("C_qka", "copy", 4)
            add("C_va", "tokens", 2)
            add("C_qkb", "copy", 4)
            add("C_vb", "tokens", 2)
            add("C_merge", "merge", 16)
            add("C_out", "store", 4, squares=True)
        for half, kt in enumerate(HALVES):
            add(f"up{f}{half}", "up", kt)
            add(f"down{f}{half}", "down", 8, kt=kt, squares=(half == 1))
    b = h = r = m = s = 0
    order = list(st.values())
    for x in order:
        assert x.blocks % 2 == 0
        x.b0, x.h0, x.r0, x.m0, x.s0 = b, h, r, m, s
        b += x.blocks
        h += x.blocks if x.kind == "up" else 0
        r += DT if x.squares else 0
        m += x.blocks // 2 if x.kind == "merge" else 0
        s += DT if x.kind in ("residual", "down", "store") else 0
    for x, y in zip(order, order[1:] + [None]):
        x.next = y
    return st


def weights_of(stage, par):
    if stage.kind == "merge":
        return SLOT if par == 0 else SLOT // 2
    return stage.kt * P if stage.kind == "down" else SLOT


class Rows:

    def __init__(self, heads, maps, causal, per_tile, lag):
        self.heads, self.maps, self.causal, self.per_tile, self.lag = heads, maps, causal, per_tile, lag
        self.units = heads * TT

    def keys(self, qt):
        return (qt + 1) * P if self.causal else S


def attentions():
    a = {"B": Rows(B_HEADS, 1, True, 2, 2), "DA": Rows(DA_HEADS, 2, False, 1, 2), "NA": Rows(NA_HEADS, 1, False, 2, 2)}
    s = u = h = y = i = 0
    for r in a.values():
        r.s0, r.u0, r.p0, r.y0, r.i0 = s, u, h, y, i
        s += r.units * r.maps
        u += r.units
        h += r.heads
        y += r.heads // r.per_tile
        i += r.units * (1 if r.maps == 1 else 3)
    return a


def build(nc, x, a_w_in, a_b_gate, a_g_head, a_w_out, b_w_q, b_rel_bias, b_w_o, kv_norm_g, w_kv,
          norm_mix_g, norm_ffn_g, ffn_w_gate, ffn_w_up, ffn_w_down, final_norm_g, pre_mix_w, w_in,
          b_gate, lambda_q1, lambda_k1, lambda_q2, lambda_k2, subln_w, rpb, w_branch_a, w_branch_b,
          w_out, post_mix_w, pre_ffn_w, w_gate, w_up, w_down, post_ffn_w, out):
    st = plan()
    att = attentions()
    with ExitStack() as ctx:
        def sem(name):
            return ctx.enter_context(nc.semaphore(name))

        def sb(name, shape, dt=F32):
            return ctx.enter_context(nc.sbuf_tensor(name, shape, dt))

        ident = sb("ident", [P, P])
        ones = sb("ones", [P, P])
        gains = sb("gains", [P, NGAIN + DT])
        ss = sb("ss", [P, S])
        rs = sb("rs", [P, S])
        rowmax = sb("rowmax", [P, P])
        rowsum = sb("rowsum", [P, P])
        rowinv = sb("rowinv", [P, P])
        lam = sb("lam", [P, 8])
        rst = sb("rst", [P, TT, 8])
        namask = sb("namask", [P, GRID_W])
        eps = sb("eps", [P, 2])
        stage = sb("stage", [P, 2, SLOT])
        wh = sb("wh", [P, 2, SLOT], F32R)
        wl = sb("wl", [P, 2, SLOT], F32R)
        res = sb("res", [P, DT, S])
        xh = sb("xh", [P, DT, S], F32R)
        xl = sb("xl", [P, DT, S], F32R)
        KB = 1024
        region_base = nc.sbuf_base
        sb("region", [P, 104 * KB // 4])

        def at(name, kb, shape, dt=F32):
            return nc.alloc_sbuf_tensor_at(name, shape, dt, offset=region_base + int(kb * KB))

        work = at("work", 64, [P, 4, S])
        hidh = at("hidh", 0, [P, 12, S], F32R)
        hidl = at("hidl", 24, [P, 12, S], F32R)
        acc = at("acc", 48, [P, DT, S])
        ss2 = at("ss2", 48, [P, S])
        x2h = at("x2h", 72, [P, DT, S], F32R)
        x2l = at("x2l", 88, [P, DT, S], F32R)
        post = at("post", 88, [P, DT, S])
        result = at("result", 72, [P, TT, D])
        xin = at("xin", 0, [P, TT, D])
        extsrc = at("extsrc", 48, [B_HEADS, N_REL])
        ext = at("ext", 51, [B_HEADS, EXT])
        rpsrc = at("rpsrc", 54, [NA_HEADS * 15, 31])
        rppad = at("rppad", 55, [NA_HEADS * 15, RPW])
        gload = at("gload", 72, [P, P])
        lrow = at("lrow", 102.5, [1, 4, DH])
        qk = at("qk", 0, [P, DT, S])
        va = at("va", 16, [P, TT, D])
        og = at("og", 32, [P, DT, S])
        pt = at("pt", 48, [P, 2, 4, S])
        wg = at("wg", 73, [P, DT, 16])
        wgh = at("wgh", 74, [P, DT, 16], F32R)
        wgl = at("wgl", 75, [P, DT, 16], F32R)
        gi = at("gi", 76, [16, S])
        gf = at("gf", 78, [A_HEADS, S])
        lf = at("lf", 80, [A_HEADS, S])
        gb = at("gb", 82, [A_HEADS, S])
        gu = at("gu", 84, [A_HEADS, S])
        gm = at("gm", 86, [A_HEADS, S])
        gn = at("gn", 88, [A_HEADS, S])
        sel = at("sel", 90, [A_HEADS, A_HEADS, P])
        ut = at("ut", 94, [P, TT, A_HEADS])
        efl = at("efl", 94.25, [P, 2, S])
        hs = at("hs", 98.25, [P, S])
        hq = at("hq", 100.25, [P, S])
        dn = at("dn", 76, [P, S])
        hr = at("hr", 78, [P, S])
        hn = at("hn", 80, [P, S])
        brow = at("brow", 102.25, [16, 1])
        bk = at("bk", 0, [P, DT, S])
        bv = at("bv", 16, [P, TT, D])
        bq = at("bq", 32, [P, DT, S])
        relt = at("relt", 72, [P, B_HEADS, S])
        cva = at("cva", 16, [P, TT, 512])
        qkb = at("qkb", 24, [P, DT, S])
        cvb = at("cvb", 40, [P, TT, 512])
        rpt = at("rpt", 72, [P, 2, NRO, GRID_W])
        darow = at("darow", 75.5, [P, 2, S])
        datmp = at("datmp", 80, [P, 2, S])
        absd = at("absd", 84, [P, 896])
        yah = at("yah", 88, [P, 4, S], F32R)
        yal = at("yal", 96, [P, 4, S], F32R)
        ybh = at("ybh", 0, [P, 4, S], F32R)
        ybl = at("ybl", 8, [P, 4, S], F32R)
        mgh = at("mgh", 16, [P, DT, S], F32R)
        mgl = at("mgl", 32, [P, DT, S], F32R)

        psum = ctx.enter_context(nc.psum_tensor("psum", [P, 8, S], F32))
        ext_dram = nc.dram_tensor("ext_scratch", [B_HEADS, EXT], F32, kind="Internal").ap()
        rp_dram = nc.dram_tensor("rp_scratch", [NA_HEADS * 15, RPW], F32, kind="Internal").ap()

        w_loaded = [sem("w_loaded0"), sem("w_loaded1")]
        w_hi, w_lo = sem("w_hi"), sem("w_lo")
        mm_done = sem("mm_done")
        block_out = sem("block_out")
        n_hi, n_lo = sem("n_hi"), sem("n_lo")
        norm_sum = sem("norm_sum")
        norm_root, norm_rs, ss_zero = sem("norm_root"), sem("norm_rs"), sem("ss_zero")
        sq_src, tile_sq, ss_added = sem("sq_src"), sem("tile_sq"), sem("ss_added")
        tile_sq2, ss2_added, fin_step, fin_root, fin_res = (
            sem(n) for n in ("tile_sq2", "ss2_added", "fin_step", "fin_root", "fin_res"))
        rst_t, rst_ready, h_in, o_out = sem("rst_t"), sem("rst_ready"), sem("h_in"), sem("o_out")
        h_sig, h_act, h_full, h_hi, h_lo = sem("h_sig"), sem("h_act"), sem("h_full"), sem("h_hi"), sem("h_lo")
        m_sig, m_a, m_sum, m_hi, m_lo = sem("m_sig"), sem("m_a"), sem("m_sum"), sem("m_hi"), sem("m_lo")
        x_in, small_in, gate_in = sem("x_in"), sem("small_in"), sem("gate_in")
        tab_in, tab_step, tab_out = sem("tab_in"), sem("tab_step"), sem("tab_out")
        relt_in, relt_ready = sem("relt_in"), sem("relt_ready")
        rpt_in, rpt_ready = [sem("rpt_in0"), sem("rpt_in1")], sem("rpt_ready")
        const = sem("const")
        gain_t, gain_out, gain_ready = sem("gain_t"), sem("gain_out"), sem("gain_ready")
        xt_done, xt_out = sem("xt_done"), sem("xt_out")
        wg_hi, wg_lo, g_done, g_step, g_act = sem("wg_hi"), sem("wg_lo"), sem("g_done"), sem("g_step"), sem("g_act")
        gf_in, u_t, u_ready = sem("gf_in"), sem("u_t"), sem("u_ready")
        lam_step, lam_exp, lam_mm = sem("lam_step"), sem("lam_exp"), sem("lam_mm")
        a_mrow, a_floor, a_s, a_d, a_mask, a_p = (sem(n) for n in ("a_mrow", "a_floor", "a_s", "a_d", "a_mask", "a_p"))
        a_den, a_abs, a_step, a_sq, a_ss, a_ln, a_rs, a_gated, a_hi, a_lo = (
            sem(n) for n in ("a_den", "a_abs", "a_step", "a_sq", "a_ss", "a_ln", "a_rs", "a_gated", "a_hi", "a_lo"))
        s_done, s_biased, s_exp, s_inv, s_prob = (sem(n) for n in ("s_done", "s_biased", "s_exp", "s_inv", "s_prob"))
        t_done, t_out, pv_done, y_hi, y_lo = (sem(n) for n in ("t_done", "t_out", "pv_done", "y_hi", "y_lo"))
        d_sq, d_ss, d_ln, d_rs, d_full, absd_ready, absd_scaled = (
            sem(n) for n in ("d_sq", "d_ss", "d_ln", "d_rs", "d_full", "absd_ready", "absd_scaled"))
        post_scaled, rt_done, rt_out, post_ready, tok_rs, ot_done, ot_out, stored = (
            sem(n) for n in ("post_scaled", "rt_done", "rt_out", "post_ready", "tok_rs", "ot_done", "ot_out", "stored"))

        EVENT = {"x": 0, "A_out": 1, "down01": 2, "B_out": 3, "down11": 4, "C_out": 5, "post_mix": 6, "down21": 7}
        SPLIT = {"x": (0, xh, xl, MIX0), "A_out": (1, x2h, x2l, FFN0), "down01": (2, xh, xl, KVN),
                 "mix1": (3, xh, xl, MIX1), "B_out": (4, x2h, x2l, FFN1), "down11": (5, xh, xl, FINPRE),
                 "post_mix": (6, xh, xl, PREFFN)}

        def row_buffer(which, u, m, n):
            if which == "DA":
                return darow[:, m, 0:n] if u % 3 == 2 else work[:, 2 * (u % 3) + m, 0:n]
            return work[:, u % 4, 0:n]

        def first_bank(name, i, par):
            if name in ("A_out", "B_out", "C_merge") and par == 0 and isinstance(i, int) and i == 0:
                return 4
            return 2 * par

        block = ctx.enter_context(nc.Block())

        def run_pairs(eng, stage_, step, start):
            n = stage_.blocks // 2 - 1
            if n - start > 1:
                with eng.Fori(start, n) as j:
                    step(j, 0)
                    step(j, 1)
            else:
                for j in range(start, n):
                    step(j, 0)
                    step(j, 1)

        @block.sync
        def _(sp):
            def sources(name, i):
                s = st[name]

                def cols(w, c, n):
                    return w[:, bass.ds(c, n)].rearrange("(k p) n -> p k n", p=P)

                if s.kind == "up":
                    f = int(name[2])
                    g = ffn_w_gate[f] if f < 2 else w_gate[0]
                    u = ffn_w_up[f] if f < 2 else w_up[0]
                    c = HALVES[0] * P * int(name[3])
                    return [cols(g, i * P + c, P), cols(u, i * P + c, P)], (DT, P)
                if s.kind == "down":
                    f, half = int(name[4]), int(name[5])
                    w = ffn_w_down[f] if f < 2 else w_down[0]
                    r, k = HALVES[0] * P * half, s.kt // 2 * P
                    return [cols(w[r:r + k, :], i * P, P), cols(w[r + k:r + 2 * k, :], i * P, P)], (s.kt // 2, P)
                w, c = {"A_qk": (a_w_in[0], 0), "A_v": (a_w_in[0], 1024), "A_o": (a_w_in[0], 2048),
                        "A_out": (a_w_out[0], 0), "B_k": (w_kv, 0), "B_v": (w_kv, 1024), "B_q": (b_w_q[0], 0),
                        "B_out": (b_w_o[0], 0), "C_qka": (w_in[0], 0), "C_va": (w_in[0], 1024),
                        "C_qkb": (w_in[0], 1536), "C_vb": (w_in[0], 2560), "C_out": (w_out[0], 0)}[name]
                k = DT // 2 * P
                return [cols(w[0:k, :], i * 256 + c, 256), cols(w[k:2 * k, :], i * 256 + c, 256)], (DT // 2, 256)

            def merge_sources(j, par):
                def cols(w, c):
                    return w[:, bass.ds(c, P)].rearrange("(k p) n -> p k n", p=P)

                if par == 0:
                    return [cols(w_in[0], j * P + 3072), cols(w_in[0], j * P + 4096)], (DT, P)
                return [cols(w_branch_a[0], j * P), cols(w_branch_b[0], j * P)], (4, P)

            def load(s, name, j, par):
                b = s.b0 + 2 * j + par
                if s.kind == "merge":
                    if par == 0:
                        sp.wait_ge(w_lo, b)
                elif not isinstance(b, int) or b >= 2:
                    sp.wait_ge(w_lo, b - 1)
                src, (k, n) = merge_sources(j, par) if s.kind == "merge" else sources(name, 2 * j + par)
                dst = stage[:, par, 0:2 * k * n].rearrange("p (a k n) -> p a k n", a=2, k=k)
                for a in range(2):
                    sp.dma_start(dst[:, a], src[a]).then_inc(w_loaded[par], 16)

            def load_neighbour_biases():
                for h in range(NA_HEADS):
                    if h == 0:
                        sp.wait_ge(s_biased, att["DA"].s0)
                    elif h == 1:
                        sp.wait_ge(t_done, att["NA"].u0)
                    else:
                        sp.wait_ge(s_biased, att["NA"].s0 + TT * (h - 1))
                    for half in range(2):
                        src = bass.AP(rp_dram.tensor, (15 * h + 1 - half) * RPW,
                                      [[1, GRID_W], [RPW, NRO], [1, GRID_W]])
                        sp.dma_start(rpt[64 * half:64 * half + 64, h % 2], src).then_inc(rpt_in[h % 2], 16)

            def load_stage(name):
                s = st[name]
                if s.kind == "merge":
                    load(s, name, 0, 0)
                    load(s, name, 0, 1)
                    load_neighbour_biases()
                    with nc.sync.Fori(1, s.blocks // 2) as j:
                        load(s, name, j, 0)
                        load(s, name, j, 1)
                    return
                if s.b0 == 0 or s.blocks == 2:
                    for j in range(s.blocks // 2):
                        load(s, name, j, 0)
                        load(s, name, j, 1)
                else:
                    with nc.sync.Fori(0, s.blocks // 2) as j:
                        load(s, name, j, 0)
                        load(s, name, j, 1)

            for t in range(TT):
                sp.dma_start(xin[:, t, :], x[0, t * P:(t + 1) * P, :]).then_inc(x_in, 16)
            vectors = [(MIX0, norm_mix_g[0]), (FFN0, norm_ffn_g[0]), (KVN, kv_norm_g), (MIX1, norm_mix_g[1]),
                       (FFN1, norm_ffn_g[1]), (FINAL, final_norm_g), (PREMIX, pre_mix_w[0]),
                       (POSTMIX, post_mix_w[0]), (PREFFN, pre_ffn_w[0]), (POSTFFN, post_ffn_w[0]),
                       (GHEAD, a_g_head[0]), (BGATE2, b_gate[0]), (SUBLN, subln_w[0])]
            for row, v in vectors:
                n = v.shape[0] // P
                sp.dma_start(gload[row:row + n, :], v.rearrange("(a b) -> a b", b=P)).then_inc(small_in, 16)
            sp.dma_start(brow[:, :], a_b_gate[0].rearrange("(a b) -> a b", b=1)).then_inc(small_in, 16)
            for i, v in enumerate((lambda_q1, lambda_k1, lambda_q2, lambda_k2)):
                sp.dma_start(lrow[0:1, i, :], v).then_inc(small_in, 16)
            sp.dma_start(wg[:, :, :], a_w_in[0, :, 3072:3088].rearrange("(k p) n -> p k n", p=P)).then_inc(gate_in, 16)
            sp.dma_start(extsrc[:, :], b_rel_bias[0]).then_inc(tab_in, 16)
            sp.dma_start(rpsrc[:, :], rpb[0].rearrange("h a b -> (h a) b")).then_inc(tab_in, 16)
            load(st["A_qk"], "A_qk", 0, 0)
            load(st["A_qk"], "A_qk", 0, 1)
            sp.wait_ge(tab_step, 3)
            sp.dma_start(ext_dram, ext[:, :]).then_inc(tab_out, 16)
            sp.dma_start(rp_dram, rppad[:, :]).then_inc(tab_out, 16)
            sp.wait_ge(tab_out, 32)
            load(st["A_qk"], "A_qk", 1, 0)
            load(st["A_qk"], "A_qk", 1, 1)

            for name in list(st)[1:]:
                load_stage(name)
                if name == "down01":
                    sp.wait_ge(mm_done, st["down01"].b0)
                    src = bass.AP(ext_dram.tensor, 0, [[1, P], [EXT, B_HEADS], [1, S]])
                    sp.dma_start(relt[:, :, :], src).then_inc(relt_in, 16)
            out_t = out[0].rearrange("(t p) d -> p t d", p=P)
            for t in range(TT):
                sp.wait_ge(ot_out, 2 * (t + 1))
                sp.dma_start(out_t[:, t, :], result[:, t, :]).then_inc(stored, 16)
            sp.wait_ge(stored, 16 * TT)

        @block.gpsimd
        def _(pool):
            nc.gpsimd.memset(ones[:, :], 1.0).then_inc(const, 1)
            nc.gpsimd.memset(sel[:, :, :], 1.0).then_inc(const, 1)
            nc.gpsimd.memset(rppad[:, :], 0.0).then_inc(const, 1)
            nc.gpsimd.memset(namask[:, :], 0.0).then_inc(const, 1)
            nc.gpsimd.memset(eps[:, 0:1], D * EPS).then_inc(const, 1)
            nc.gpsimd.memset(eps[:, 1:2], A_DV * EPS).then_inc(const, 1)
            pool.wait_ge(const, 6)
            nc.gpsimd.affine_select(out=ident[:, :], in_=ones[:, :], compare_op=ALU.is_equal, fill=0.0,
                                    base=0, pattern=[[-1, P]], channel_multiplier=1).then_inc(const, 1)
            nc.gpsimd.affine_select(out=sel[:, :, :], in_=sel[:, :, :], compare_op=ALU.is_equal, fill=0.0,
                                    base=0, pattern=[[-1, A_HEADS], [0, P]], channel_multiplier=1).then_inc(const, 1)
            for half in range(2):
                pool.wait_ge(const, 8 + half)
                m = namask[64 * half:64 * half + 64, 16:64]
                nc.gpsimd.affine_select(out=m, in_=m, compare_op=ALU.is_ge, fill=UP * NEG,
                                        base=GRID_W - 1 - 16 + NA_COLS // 2, pattern=[[-1, 48]],
                                        channel_multiplier=-1).then_inc(const, 1)
            for half in range(2):
                pool.wait_ge(const, 10 + half)
                m = namask[64 * half:64 * half + 64, 0:48]
                nc.gpsimd.affine_select(out=m, in_=m, compare_op=ALU.is_ge, fill=UP * NEG,
                                        base=NA_COLS // 2 - 1 - (GRID_W - 1), pattern=[[1, 48]],
                                        channel_multiplier=1).then_inc(const, 1)
            pool.wait_ge(const, 12)
            for g in range(A_HEADS * TT):
                pool.wait_ge(a_d, g + 1)
                d = work[:, g % TT, 0:P]
                nc.gpsimd.affine_select(out=d, in_=d, compare_op=ALU.is_ge, fill=0.0, base=0,
                                        pattern=[[1, P]], channel_multiplier=-1).then_inc(a_mask, 1)
            pool.wait_ge(relt_in, 16)
            pool.wait_ge(a_mask, A_HEADS * TT)
            nc.gpsimd.memset(relt[0:CHUNK, :, 0:CHUNK], UP * NEG).then_inc(relt_ready, 1)
            pool.wait_ge(relt_ready, 1)
            pool.wait_ge(s_biased, att["DA"].s0)
            pool.wait_ge(mm_done, st["down11"].b0)
            nc.gpsimd.iota(absd[:, :], pattern=[[2, 896]], base=-768, channel_multiplier=-2,
                           allow_small_or_imprecise_dtypes=True).then_inc(absd_ready, 1)
            for h in range(NA_HEADS):
                pool.wait_ge(rpt_in[h % 2], 32 * (h // 2 + 1))
                pool.wait_ge(const, 12)
                r = rpt[:, h % 2]
                nc.gpsimd.tensor_tensor(r, r, namask[:, :].unsqueeze(1).to_broadcast([P, NRO, GRID_W]),
                                        ALU.add).then_inc(rpt_ready, 1)

        @block.scalar
        def _(act):
            def split(pair, b, par, n):
                act.wait_ge(w_loaded[par], (pair + 1) * 32)
                if not isinstance(b, int) or b >= 2:
                    act.wait_ge(mm_done, b - 1)
                nc.scalar.copy(wh[:, par, 0:n], stage[:, par, 0:n]).then_inc(w_hi, 1)

            def part_hi(which, t, src):
                n, hi, lo, gain = SPLIT[which]
                nc.scalar.activation(hi[:, bass.ds(t, 1), :], src, ACT.Identity,
                                     scale=gains[:, bass.ds(t + gain, 1)]).then_inc(n_hi, 1)

            def outputs(name, b, i, par):
                two = st[name].kind != "down"
                act.wait_ge(block_out, b + 1)
                for a in range(2 if two else 1):
                    t = 2 * i + a if two else i
                    buf = 2 * par + a if two else par
                    tile = (acc if name in ("C_out", "down21") else res)[:, bass.ds(t, 1), :]
                    act.wait_ge(ss_added, t + 8 * EVENT[name] - (3 if two else 1))
                    if name == "down11" and (not isinstance(t, int) or t >= 2):
                        act.wait_ge(ss2_added, t - 1)
                    if name in SPLIT:
                        part_hi(name, t, tile)
                    nc.scalar.activation(work[:, buf:buf + 1, :], tile, ACT.Square).then_inc(tile_sq, 1)
                    if name == "down21":
                        nc.scalar.activation(post[:, bass.ds(t, 1), :], tile, ACT.Identity,
                                             scale=gains[:, bass.ds(t + POSTFFN, 1)]).then_inc(post_ready, 1)
                    if name == "down11":
                        nc.scalar.activation(work[:, 2 + par:3 + par, :], tile, ACT.Square,
                                             scale=gains[:, bass.ds(t + FINAL, 1)]).then_inc(tile_sq2, 1)

            def epilogue(name, b, i, par):
                s = st[name]
                if s.kind == "sigmoid":
                    act.wait_ge(block_out, b + 1)
                    nc.scalar.activation(og[:, bass.ds(i * 2, 2), :], work[:, 2 * par:2 * par + 2, :],
                                         ACT.Sigmoid).then_inc(o_out, 1)
                elif s.kind == "up":
                    t = s.h0 + i
                    act.wait_ge(h_in, t + 1)
                    nc.scalar.activation(work[:, 1, :], work[:, 0, :], ACT.Sigmoid).then_inc(h_sig, 1)
                    act.wait_ge(h_full, t + 1)
                    nc.scalar.copy(hidh[:, bass.ds(i, 1), :], work[:, 2 + par:3 + par, :]).then_inc(h_hi, 1)
                elif s.squares:
                    outputs(name, b, i, par)

            def merge_epilogue(s, b, j, par):
                if par == 0:
                    act.wait_ge(block_out, b + 1)
                    nc.scalar.activation(work[:, 0, :], work[:, 0, :], ACT.Sigmoid,
                                         bias=gains[:, bass.ds(j + BGATE2, 1)]).then_inc(m_sig, 1)
                    nc.scalar.activation(work[:, 1, :], work[:, 1, :], ACT.Sigmoid,
                                         bias=gains[:, bass.ds(j + BGATE2 + DT, 1)]).then_inc(m_sig, 1)
                else:
                    act.wait_ge(m_sum, s.m0 + j + 1)
                    nc.scalar.copy(mgh[:, bass.ds(j, 1), :], work[:, 2:3, :]).then_inc(m_hi, 1)

            def linear(name, norm=None):
                s = st[name]

                def step(j, par):
                    b = s.b0 + 2 * j + par
                    split(s.b0 // 2 + j + par, b + 1, 1 - par, weights_of(s, 1 - par))
                    if norm and isinstance(j, int) and j == par == 0:
                        norm()
                    finish(j, par)

                def finish(j, par):
                    b = s.b0 + 2 * j + par
                    if s.kind == "merge":
                        if par == 1:
                            merge_epilogue(s, b - 1, j, 0)
                            merge_epilogue(s, b, j, 1)
                    else:
                        epilogue(name, b, 2 * j + par, par)

                last = s.blocks // 2 - 1
                if last:
                    step(0, 0)
                    step(0, 1)
                run_pairs(nc.scalar, s, step, 1)
                step(last, 0)
                if s.next:
                    split(s.next.b0 // 2, s.next.b0, 0, weights_of(s.next, 0))
                finish(last, 1)

            def root(k):
                act.wait_ge(norm_sum, k + 1)
                nc.scalar.activation(rs[:, :], psum[:, 4, :], ACT.Sqrt, bias=eps[:, 0:1]).then_inc(norm_root, 1)

            def feed_forward(f):
                def norm():
                    root((1, 3, 6)[f])
                    nc.scalar.preload_act_table(ACT.Sigmoid)

                linear(f"up{f}0", norm)
                linear(f"down{f}0")
                if f == 2:
                    for i in range(2 * TT):
                        t, a = divmod(i, 2)
                        act.wait_ge(rt_done, i + 1)
                        nc.scalar.copy(result[:, t, 512 * a:512 * a + 512], psum[:, 4 + i % 2, :]).then_inc(rt_out, 1)
                linear(f"up{f}1")
                nc.scalar.preload_act_table(ACT.Sqrt)
                linear(f"down{f}1")

            def rows_of_rs(n):
                act.wait_ge(rst_t, n + 1)
                nc.scalar.copy(rst[:, :, :], psum[:, 6, 0:TT * 8].rearrange("p (t h) -> p t h", t=TT)).then_inc(rst_ready, 1)

            def softmax(which, yh):
                r = att[which]
                for t in range(r.units + r.lag + 5):
                    if t < r.units:
                        for m in range(r.maps):
                            g = r.s0 + t * r.maps + m
                            row = row_buffer(which, t, m, r.keys(t % TT))
                            act.wait_ge(s_biased, g + 1)
                            nc.scalar.activation(row, row, ACT.Exp, bias=rowmax[:, g:g + 1], scale=-1.0,
                                                 accum_out=rowsum[:, g:g + 1]).then_inc(s_exp, 1)
                    u = t - r.lag
                    if 0 <= u < r.units:
                        h, qt = divmod(u, TT)
                        n = r.keys(qt) // P
                        act.wait_ge(t_done, r.u0 + u + 1)
                        if h >= 2:
                            act.wait_ge(pv_done, r.p0 + h - 1)
                        nc.scalar.copy(pt[:, h % 2, 0:n, qt * P:(qt + 1) * P],
                                       psum[:, 6 + (r.u0 + u) % 2, 0:n * P].rearrange("p (k q) -> p k q", q=P)
                                       ).then_inc(t_out, 1)
                    u = t - r.lag - 2
                    if 0 <= u < r.units and u % TT == TT - 1 and (u // TT + 1) % r.per_tile == 0:
                        y = r.y0 + (u // TT) // r.per_tile
                        act.wait_ge(pv_done, r.p0 + u // TT + 1)
                        if which == "DA":
                            nc.scalar.activation(datmp[:, 0, :], psum[:, y % 2, :], ACT.Square).then_inc(d_sq, 1)
                        else:
                            nc.scalar.copy(yh[:, y - r.y0, :], psum[:, y % 2, :]).then_inc(y_hi, 1)
                    u = t - r.lag - 4
                    if which == "DA" and 0 <= u < r.units and u % TT == TT - 1:
                        act.wait_ge(d_ss, u // TT + 1)
                        nc.scalar.activation(datmp[:, 0, :], psum[:, 2 + (r.y0 + u // TT) % 2, :], ACT.Ln,
                                             bias=eps[:, 1:2]).then_inc(d_ln, 1)
                        act.wait_ge(d_ln, u // TT + 1)
                        nc.scalar.activation(datmp[:, 0, :], datmp[:, 0, :], ACT.Exp, scale=-0.5).then_inc(d_rs, 1)
                        act.wait_ge(d_full, u // TT + 1)
                        nc.scalar.copy(yh[:, u // TT, :], datmp[:, 1, :]).then_inc(y_hi, 1)

            for t in range(2):
                act.wait_ge(xt_done, t + 1)
                nc.scalar.copy(res[:, t, :], psum[:, 4 + t, :]).then_inc(xt_out, 1)
            act.wait_ge(gain_t, 1)
            nc.scalar.copy(gains[:, 0:NGAIN], psum[:, 7, 0:NGAIN]).then_inc(gain_out, 1)
            act.wait_ge(gate_in, 16)
            nc.scalar.copy(wgh[:, :, :], wg[:, :, :]).then_inc(wg_hi, 1)
            act.wait_ge(lam_step, 2)
            nc.scalar.activation(lam[0:1, 2:4], lam[0:1, 0:2], ACT.Exp).then_inc(lam_exp, 1)
            for t in range(DT):
                if t >= 2:
                    act.wait_ge(xt_done, t + 1)
                    nc.scalar.copy(res[:, t, :], psum[:, 4 + t % 2, :]).then_inc(xt_out, 1)
                act.wait_ge(xt_out, t + 1)
                if t == 0:
                    act.wait_ge(gain_ready, 3)
                part_hi("x", t, res[:, t:t + 1, :])
                if t >= 4:
                    act.wait_ge(ss_added, t - 3)
                nc.scalar.activation(work[:, t % 4, :], res[:, t, :], ACT.Square).then_inc(tile_sq, 1)
            split(0, 0, 0, SLOT)
            act.wait_ge(const, 6)

            def gates():
                root(0)
                act.wait_ge(g_step, 2)
                act.dma_start(gf[:, :], gi[A_HEADS:2 * A_HEADS, :]).then_inc(gf_in, 16)

            linear("A_qk", gates)
            rows_of_rs(0)
            nc.scalar.preload_act_table_set(LN_EXP)
            act.wait_ge(g_step, 3)
            nc.scalar.activation(lf[:, :], lf[:, :], ACT.Exp, scale=-1.0).then_inc(g_act, 1)
            act.wait_ge(g_act, 1)
            nc.scalar.activation(lf[:, :], lf[:, :], ACT.Ln, bias=1.0).then_inc(g_act, 1)
            nc.scalar.preload_act_table(ACT.Sigmoid)
            linear("A_v")
            linear("A_o")
            act.wait_ge(u_t, 1)
            nc.scalar.copy(ut[:, :, :], psum[:, 6, 0:TT * A_HEADS].rearrange("p (t h) -> p t h", t=TT)).then_inc(u_ready, 1)
            act.wait_ge(u_ready, 1)
            act.wait_ge(o_out, 4)
            nc.scalar.preload_act_table_set(LN_EXP)
            for h in range(A_HEADS + 2):
                if h < A_HEADS:
                    act.wait_ge(a_mrow, h + 1)
                    if h >= 2:
                        act.wait_ge(a_step, 4 * (h - 2) + 1)
                    nc.scalar.activation(efl[:, h % 2, :], psum[:, 7, :], ACT.Exp).then_inc(a_floor, 1)
                    for t in range(TT):
                        if h >= 1:
                            act.wait_ge(a_p, TT * (h - 1) + t + 1)
                        nc.scalar.activation(work[:, t, 0:S - t * P], psum[:, 6, t * P:S], ACT.Exp,
                                             bias=ut[:, t, h:h + 1], scale=-1.0).then_inc(a_d, 1)
                if h >= 2:
                    act.wait_ge(a_ss, h - 1)
                    nc.scalar.activation(hr[:, :], psum[:, 2 + h % 2, :], ACT.Ln, bias=eps[:, 1:2]).then_inc(a_ln, 1)
                    act.wait_ge(a_ln, h - 1)
                    nc.scalar.activation(hr[:, :], hr[:, :], ACT.Exp, scale=-0.5).then_inc(a_rs, 1)
                    act.wait_ge(a_gated, h - 1)
                    nc.scalar.copy(xh[:, h - 2, :], og[:, h - 2, :]).then_inc(a_hi, 1)
                if 1 <= h <= A_HEADS:
                    act.wait_ge(a_den, h)
                    nc.scalar.activation(dn[:, :], psum[:, 2 + (h - 1) % 2, :], ACT.Abs).then_inc(a_abs, 1)
                    act.wait_ge(a_step, 4 * (h - 1) + 3)
                    if h >= 2:
                        act.wait_ge(a_ss, h - 1)
                    nc.scalar.activation(hq[:, :], hs[:, :], ACT.Square).then_inc(a_sq, 1)
            linear("A_out")
            feed_forward(0)
            linear("B_k", lambda: root(2))
            rows_of_rs(1)
            linear("B_v")
            act.wait_ge(mm_done, st["B_v"].b0 + 4)
            for t in range(DT):
                part_hi("mix1", t, res[:, t:t + 1, :])
            linear("B_q")
            nc.scalar.preload_act_table(ACT.Exp)
            softmax("B", xh)
            linear("B_out")
            feed_forward(1)

            def both_norms():
                root(4)
                act.wait_ge(fin_step, 2)
                nc.scalar.activation(work[:, 0, :], work[:, 0, :], ACT.Sqrt, bias=eps[:, 0:1]).then_inc(fin_root, 1)

            linear("C_qka", both_norms)
            rows_of_rs(2)
            for name in ("C_va", "C_qkb", "C_vb"):
                linear(name)
            nc.scalar.preload_act_table_set(LN_EXP)
            softmax("DA", yah)
            softmax("NA", ybh)
            nc.scalar.preload_act_table(ACT.Sigmoid)
            linear("C_merge")
            nc.scalar.preload_act_table(ACT.Sqrt)
            linear("C_out")
            root(5)
            for t in range(DT):
                act.wait_ge(sq_src, t + 1)
                part_hi("post_mix", t, res[:, t:t + 1, :])
            for t in range(DT):
                act.wait_ge(ss_added, 8 * EVENT["post_mix"] + t - 3)
                nc.scalar.activation(work[:, t % 4, :], res[:, t, :], ACT.Square).then_inc(tile_sq, 1)
            feed_forward(2)
            act.wait_ge(norm_sum, 8)
            nc.scalar.activation(rst[:, :, :], psum[:, 4, 0:TT * 8].rearrange("p (t h) -> p t h", t=TT), ACT.Sqrt,
                                 bias=eps[:, 0:1]).then_inc(norm_root, 1)

        @block.vector
        def _(dve):
            vec = nc.vector

            def split(b, par, n):
                dve.wait_ge(w_hi, b + 1)
                vec.tensor_tensor(wl[:, par, 0:n], stage[:, par, 0:n], wh[:, par, 0:n].bitcast(F32),
                                  ALU.subtract).then_inc(w_lo, 1)

            def add_square(event, t, buf):
                dve.wait_ge(tile_sq, t + 8 * event + 1)
                dve.wait_ge(ss_zero, event + 1)
                if not isinstance(t, int) or 8 * event + t:
                    dve.wait_ge(ss_added, t + 8 * event)
                vec.tensor_tensor(ss[:, :], ss[:, :], work[:, buf, :], ALU.add).then_inc(ss_added, 1)

            def part_lo(which, t, src):
                n, hi, lo, gain = SPLIT[which]
                dve.wait_ge(n_hi, t + DT * n + 1)
                vec.scalar_tensor_tensor(out=lo[:, bass.ds(t, 1), :], in0=src, scalar=gains[:, bass.ds(t + gain, 1)],
                                         in1=hi[:, bass.ds(t, 1), :].bitcast(F32),
                                         op0=ALU.mult, op1=ALU.subtract).then_inc(n_lo, 1)

            def outputs(name, i, par, two):
                for a in range(2 if two else 1):
                    t = 2 * i + a if two else i
                    if name in SPLIT:
                        part_lo(name, t, res[:, bass.ds(t, 1), :])
                    add_square(EVENT[name], t, 2 * par + a if two else par)
                    if name == "down11":
                        dve.wait_ge(tile_sq2, t + 1)
                        dve.wait_ge(ss2_added, t + 1)
                        vec.tensor_tensor(ss2[:, :], ss2[:, :], work[:, 2 + par, :], ALU.add).then_inc(ss2_added, 1)

            def epilogue(name, b, i, par):
                s = st[name]
                bank = first_bank(name, i, par)
                ps = psum[:, bank:bank + 2, :]
                both = rs[:, :].unsqueeze(1).to_broadcast([P, 2, S])
                dve.wait_ge(mm_done, b + 1)
                if s.kind == "tokens":
                    if isinstance(i, int) and i == 0:
                        dve.wait_ge(rst_ready, {"A_v": 1, "B_v": 2}.get(name, 3))
                    dst = {"A_v": va, "B_v": bv, "C_va": cva, "C_vb": cvb}[name]
                    vec.tensor_tensor(dst[:, :, bass.ds(i * 256, 256)], ps.rearrange("p a (t n) -> p (a t) n", n=256),
                                      rst[:, :, 0:1].to_broadcast([P, TT, 256]), ALU.mult).then_inc(block_out, 1)
                elif s.kind == "copy":
                    dst = {"A_qk": qk, "B_k": bk, "B_q": bq, "C_qka": qk, "C_qkb": qkb}[name]
                    vec.tensor_tensor(dst[:, bass.ds(i * 2, 2), :], ps, both, ALU.mult).then_inc(block_out, 1)
                elif s.kind == "sigmoid":
                    if not isinstance(i, int) or i >= 2:
                        dve.wait_ge(o_out, i - 1)
                    vec.tensor_tensor(work[:, 2 * par:2 * par + 2, :], ps, both, ALU.mult).then_inc(block_out, 1)
                elif s.kind == "up":
                    t = s.h0 + i
                    vec.tensor_tensor(work[:, 0, :], ps[:, 0, :], rs[:, :], ALU.mult).then_inc(h_in, 1)
                    vec.tensor_tensor(work[:, 2 + par, :], ps[:, 1, :], rs[:, :], ALU.mult).then_inc(block_out, 1)
                    dve.wait_ge(h_sig, t + 1)
                    vec.tensor_tensor(work[:, 0, :], work[:, 0, :], work[:, 1, :], ALU.mult).then_inc(h_act, 1)
                    dve.wait_ge(h_act, t + 1)
                    vec.tensor_tensor(work[:, 2 + par, :], work[:, 0, :], work[:, 2 + par, :], ALU.mult).then_inc(h_full, 1)
                    dve.wait_ge(h_hi, t + 1)
                    vec.tensor_tensor(hidl[:, bass.ds(i, 1), :], work[:, 2 + par:3 + par, :],
                                      hidh[:, bass.ds(i, 1), :].bitcast(F32), ALU.subtract).then_inc(h_lo, 1)
                elif s.kind == "residual":
                    r = res[:, bass.ds(2 * i, 2), :]
                    vec.tensor_tensor(r, r, ps, ALU.add).then_inc(block_out, 1)
                    outputs(name, i, par, True)
                elif s.kind == "store":
                    vec.tensor_copy(acc[:, bass.ds(2 * i, 2), :], ps).then_inc(block_out, 1)
                    outputs(name, i, par, True)
                elif s.kind == "down":
                    f, half = int(name[4]), int(name[5])
                    r = (acc if f == 2 else res)[:, bass.ds(i, 1), :]
                    if half == 1:
                        dve.wait_ge(block_out, st[f"down{f}0"].b0 + 8)
                    if f == 2 and half == 0:
                        vec.tensor_copy(r, ps[:, 0:1, :]).then_inc(block_out, 1)
                    else:
                        vec.tensor_tensor(r, r, ps[:, 0:1, :], ALU.add).then_inc(block_out, 1)
                    if half == 1:
                        outputs(name, i, par, False)

            def merge_epilogue(s, b, j, par):
                dve.wait_ge(mm_done, b + 1)
                if par == 0:
                    bank = first_bank("C_merge", j, 0)
                    vec.tensor_tensor(work[:, 0:2, :], psum[:, bank:bank + 2, :], rs[:, :].unsqueeze(1).to_broadcast([P, 2, S]),
                                      ALU.mult).then_inc(block_out, 1)
                    return
                dve.wait_ge(m_sig, 2 * (s.m0 + j + 1))
                vec.tensor_tensor(work[:, 0, :], work[:, 0, :], psum[:, 2, :], ALU.mult).then_inc(m_a, 1)
                vec.tensor_tensor(work[:, 1, :], work[:, 1, :], psum[:, 3, :], ALU.mult).then_inc(block_out, 1)
                dve.wait_ge(m_a, s.m0 + j + 1)
                dve.wait_ge(block_out, b + 1)
                vec.tensor_tensor(work[:, 2, :], work[:, 0, :], work[:, 1, :], ALU.add).then_inc(m_sum, 1)
                dve.wait_ge(m_hi, s.m0 + j + 1)
                vec.tensor_tensor(mgl[:, bass.ds(j, 1), :], work[:, 2:3, :],
                                  mgh[:, bass.ds(j, 1), :].bitcast(F32), ALU.subtract).then_inc(m_lo, 1)

            def linear(name, norm=None):
                s = st[name]

                def step(j, par):
                    split(s.b0 + 2 * j + par + 1, 1 - par, weights_of(s, 1 - par))
                    if norm and isinstance(j, int) and j == par == 0:
                        norm()
                    finish(j, par)

                def finish(j, par):
                    b = s.b0 + 2 * j + par
                    if s.kind == "merge":
                        merge_epilogue(s, b, j, par)
                    else:
                        epilogue(name, b, 2 * j + par, par)

                last = s.blocks // 2 - 1
                if last:
                    step(0, 0)
                    step(0, 1)
                run_pairs(vec, s, step, 1)
                step(last, 0)
                if s.next:
                    split(s.next.b0, 0, weights_of(s.next, 0))
                finish(last, 1)

            def norm_scale(k):
                dve.wait_ge(norm_root, k + 1)
                vec.reciprocal(rs[:, :], rs[:, :]).then_inc(norm_rs, 1)
                vec.memset(ss[:, :], 0.0).then_inc(ss_zero, 1)
                dve.wait_ge(norm_rs, k + 1)

            def feed_forward(f):
                linear(f"up{f}0", lambda: norm_scale((1, 3, 6)[f]))
                linear(f"down{f}0")
                linear(f"up{f}1")
                if f == 1:
                    vec.memset(ss2[:, :], 0.0).then_inc(ss2_added, 1)
                linear(f"down{f}1")

            def softmax(which, yh, yl):
                r = att[which]
                for t in range(r.units + r.lag + 5):
                    if t < r.units:
                        h, qt = divmod(t, TT)
                        n = r.keys(qt)
                        for m in range(r.maps):
                            g = r.s0 + t * r.maps + m
                            row = row_buffer(which, t, m, n)
                            scores = psum[:, 4 + g % 2, 0:n]
                            if which == "B":
                                bias = relt[:, h, n - 1::-1] if n == S else relt[:, h, 0:n][:, ::-1]
                            elif which == "DA":
                                bias = absd[:, 384 - qt * P:384 - qt * P + S]
                                dve.wait_ge(absd_scaled, h + 1)
                            else:
                                ro = 6 - 2 * qt
                                bias = rpt[:, h % 2, ro:ro + 8, ::-1]
                                row = row.rearrange("p (a b) -> p a b", b=GRID_W)
                                scores = scores.rearrange("p (a b) -> p a b", b=GRID_W)
                                dve.wait_ge(rpt_ready, h + 1)
                            dve.wait_ge(s_done, g + 1)
                            back = t - (3 if which == "DA" else 4)
                            dve.wait_ge(t_done, r.u0 + max(back + 1, 0))
                            vec.tensor_tensor_reduce(row, scores, bias, -SCALE, 3e38, ALU.add, ALU.min,
                                                     rowmax[:, g:g + 1]).then_inc(s_biased, 1)
                        if which == "DA" and qt == TT - 1 and h < r.heads - 1:
                            dve.wait_ge(s_biased, r.s0 + (t + 1) * r.maps)
                            vec.tensor_scalar(absd[:, :], absd[:, :], 0.25, None, ALU.mult).then_inc(absd_scaled, 1)
                    u = t - 1
                    if 0 <= u < r.units:
                        g = r.s0 + u * r.maps
                        n = r.keys(u % TT)
                        dve.wait_ge(s_exp, g + r.maps)
                        vec.reciprocal(rowinv[:, g:g + r.maps], rowsum[:, g:g + r.maps]).then_inc(s_inv, 1)
                        row = row_buffer(which, u, 0, n)
                        if r.maps == 1:
                            dve.wait_ge(s_inv, r.i0 + u + 1)
                            vec.tensor_scalar(row, row, rowinv[:, g:g + 1], None, ALU.mult).then_inc(s_prob, 1)
                        else:
                            dve.wait_ge(s_inv, r.i0 + 3 * u + 1)
                            vec.tensor_scalar(rowinv[:, g + 1:g + 2], rowinv[:, g + 1:g + 2], lam[:, 5:6], None,
                                              ALU.mult).then_inc(s_inv, 1)
                            vec.tensor_scalar(row, row, rowinv[:, g:g + 1], None, ALU.mult).then_inc(s_inv, 1)
                            dve.wait_ge(s_inv, r.i0 + 3 * u + 3)
                            vec.scalar_tensor_tensor(out=row, in0=row_buffer(which, u, 1, n),
                                                     scalar=rowinv[:, g + 1:g + 2], in1=row,
                                                     op0=ALU.mult, op1=ALU.add).then_inc(s_prob, 1)
                    u = t - r.lag - (4 if which == "DA" else 3)
                    if 0 <= u < r.units and u % TT == TT - 1 and (u // TT + 1) % r.per_tile == 0:
                        y = r.y0 + (u // TT) // r.per_tile
                        if which == "DA":
                            h = u // TT
                            dve.wait_ge(d_rs, h + 1)
                            dve.wait_ge(y_lo, y)
                            vec.scalar_tensor_tensor(out=datmp[:, 1, :], in0=psum[:, y % 2, :],
                                                     scalar=gains[:, SUBLN:SUBLN + 1], in1=datmp[:, 0, :],
                                                     op0=ALU.mult, op1=ALU.mult).then_inc(d_full, 1)
                            dve.wait_ge(y_hi, y + 1)
                            vec.tensor_tensor(yl[:, h, :], datmp[:, 1, :], yh[:, h, :].bitcast(F32),
                                              ALU.subtract).then_inc(y_lo, 1)
                        else:
                            dve.wait_ge(y_hi, y + 1)
                            vec.tensor_tensor(yl[:, y - r.y0, :], psum[:, y % 2, :], yh[:, y - r.y0, :].bitcast(F32),
                                              ALU.subtract).then_inc(y_lo, 1)

            vec.memset(ss[:, :], 0.0).then_inc(ss_zero, 1)
            dve.wait_ge(gain_out, 1)
            vec.tensor_scalar(gains[:, 0:GHEAD], gains[:, 0:GHEAD], math.sqrt(D), None, ALU.mult).then_inc(gain_ready, 1)
            vec.tensor_scalar(gains[:, GHEAD:BGATE2], gains[:, GHEAD:BGATE2], math.sqrt(A_DV), None,
                              ALU.mult).then_inc(gain_ready, 1)
            vec.tensor_scalar(gains[:, SUBLN:NGAIN], gains[:, SUBLN:NGAIN], (1.0 - LAMBDA_INIT) * math.sqrt(2 * DH),
                              None, ALU.mult).then_inc(gain_ready, 1)
            dve.wait_ge(gain_ready, 3)
            vec.tensor_tensor(gains[:, FINPRE:FINPRE + DT], gains[:, FINAL:FINAL + DT], gains[:, PREMIX:PREMIX + DT],
                              ALU.mult).then_inc(gain_ready, 1)
            dve.wait_ge(wg_hi, 1)
            vec.tensor_tensor(wgl[:, :, :], wg[:, :, :], wgh[:, :, :].bitcast(F32), ALU.subtract).then_inc(wg_lo, 1)
            for i in range(2):
                vec.tensor_tensor_reduce(lrow[0:1, 2 * i, :], lrow[0:1, 2 * i, :], lrow[0:1, 2 * i + 1, :], 1.0, 0.0,
                                         ALU.mult, ALU.add, lam[0:1, i:i + 1]).then_inc(lam_step, 1)
            dve.wait_ge(lam_exp, 1)
            vec.tensor_tensor(lam[0:1, 4:5], lam[0:1, 3:4], lam[0:1, 2:3], ALU.subtract).then_inc(lam_step, 1)
            dve.wait_ge(lam_step, 3)
            vec.tensor_scalar(lam[0:1, 4:5], lam[0:1, 4:5], -LAMBDA_INIT, None, ALU.add).then_inc(lam_step, 1)
            dve.wait_ge(tab_in, 32)
            first = MAX_REL - (P - 1)
            vec.tensor_scalar(ext[:, 0:N_REL - first], extsrc[:, first:N_REL], UP, None, ALU.mult).then_inc(tab_step, 1)
            dve.wait_ge(tab_step, 1)
            vec.tensor_copy(ext[:, N_REL - first:EXT],
                            ext[:, N_REL - first - 1:N_REL - first].to_broadcast([B_HEADS, EXT - N_REL + first])
                            ).then_inc(tab_step, 1)
            dve.wait_ge(const, 6)
            vec.tensor_scalar(rppad[:, 48:79], rpsrc[:, ::-1], UP, None, ALU.mult).then_inc(tab_step, 1)
            for t in range(DT):
                part_lo("x", t, res[:, t:t + 1, :])
                add_square(0, t, t % 4)
            dve.wait_ge(lam_mm, 1)
            vec.tensor_copy(lam[:, 5:6], psum[:, 6, 0:1]).then_inc(lam_step, 1)
            split(0, 0, SLOT)

            def gates():
                norm_scale(0)
                dve.wait_ge(g_done, 1)
                vec.tensor_tensor(gi[:, :], psum[0:16, 7, :], rs[0:16, :], ALU.mult).then_inc(g_step, 1)
                dve.wait_ge(g_step, 1)
                vec.tensor_scalar(gi[:, :], gi[:, :], brow[:, 0:1], None, ALU.add).then_inc(g_step, 1)

            linear("A_qk", gates)
            dve.wait_ge(gf_in, 16)
            vec.scalar_tensor_tensor(out=lf[:, :], in0=gf[:, :], scalar=-1.0, in1=gf[:, :],
                                     op0=ALU.mult, op1=ALU.max).then_inc(g_step, 1)
            vec.tensor_scalar(gf[:, :], gf[:, :], 0.0, None, ALU.min).then_inc(g_step, 1)
            linear("A_v")
            dve.wait_ge(g_act, 2)
            dve.wait_ge(g_step, 4)
            vec.tensor_tensor(lf[:, :], gf[:, :], lf[:, :], ALU.subtract).then_inc(g_step, 1)
            dve.wait_ge(g_step, 5)
            vec.tensor_tensor_scan(gb[:, :], ones[0:A_HEADS, 0:1].to_broadcast([A_HEADS, S]), lf[:, :], 0.0,
                                   ALU.mult, ALU.add).then_inc(g_step, 1)
            dve.wait_ge(g_step, 6)
            vec.tensor_tensor(gu[:, :], gi[0:A_HEADS, :], gb[:, :], ALU.subtract).then_inc(g_step, 1)
            dve.wait_ge(g_step, 7)
            vec.tensor_tensor_scan(gm[:, :], gu[:, :], gu[:, :], NEG, ALU.max, ALU.max).then_inc(g_step, 1)
            dve.wait_ge(g_step, 8)
            vec.scalar_tensor_tensor(out=gn[:, :], in0=gb[:, :], scalar=-1.0, in1=gm[:, :],
                                     op0=ALU.mult, op1=ALU.subtract).then_inc(g_step, 1)
            linear("A_o")
            dve.wait_ge(o_out, 4)

            def probabilities(h, tiles):
                for t in tiles:
                    g = TT * h + t
                    dve.wait_ge(a_s, g + 1)
                    dve.wait_ge(a_mask, g + 1)
                    if h >= 2:
                        dve.wait_ge(a_den, h - 1)
                    n = S - t * P
                    vec.scalar_tensor_tensor(out=pt[:, h % 2, t, 0:n], in0=psum[:, 4 + g % 2, 0:n], scalar=SCALE,
                                             in1=work[:, t, 0:n], op0=ALU.mult, op1=ALU.mult).then_inc(a_p, 1)

            for h in range(A_HEADS + 2):
                if h < A_HEADS:
                    probabilities(h, (0, 1))
                if h >= 2:
                    e = h - 2
                    dve.wait_ge(a_rs, e + 1)
                    dve.wait_ge(a_step, 4 * e + 3)
                    vec.scalar_tensor_tensor(out=hn[:, :], in0=hs[:, :], scalar=gains[:, GHEAD + e:GHEAD + e + 1],
                                             in1=hr[:, :], op0=ALU.mult, op1=ALU.mult).then_inc(a_step, 1)
                    dve.wait_ge(a_step, 4 * e + 4)
                    vec.tensor_tensor(og[:, e, :], og[:, e, :], hn[:, :], ALU.mult).then_inc(a_gated, 1)
                if h < A_HEADS:
                    probabilities(h, (2, 3))
                if 1 <= h <= A_HEADS:
                    e = h - 1
                    dve.wait_ge(a_abs, e + 1)
                    vec.tensor_tensor(dn[:, :], dn[:, :], efl[:, e % 2, :], ALU.max).then_inc(a_step, 1)
                    dve.wait_ge(a_step, 4 * e + 1)
                    vec.reciprocal(dn[:, :], dn[:, :]).then_inc(a_step, 1)
                    dve.wait_ge(a_step, 4 * e + 2)
                    vec.tensor_tensor(hs[:, :], psum[:, e % 2, :], dn[:, :], ALU.mult).then_inc(a_step, 1)
                if h >= 2:
                    e = h - 2
                    dve.wait_ge(a_hi, e + 1)
                    vec.tensor_tensor(xl[:, e, :], og[:, e, :], xh[:, e, :].bitcast(F32), ALU.subtract).then_inc(a_lo, 1)
            linear("A_out")
            feed_forward(0)
            linear("B_k", lambda: norm_scale(2))
            linear("B_v")
            for t in range(DT):
                part_lo("mix1", t, res[:, t:t + 1, :])
            linear("B_q")
            dve.wait_ge(relt_ready, 1)
            softmax("B", xh, xl)
            linear("B_out")
            feed_forward(1)

            def both_norms():
                norm_scale(4)
                w = work[:, 0, :]
                vec.tensor_tensor(w, psum[:, 5, :], rs[:, :], ALU.mult).then_inc(fin_step, 1)
                dve.wait_ge(fin_step, 1)
                vec.tensor_tensor(w, w, rs[:, :], ALU.mult).then_inc(fin_step, 1)
                vec.tensor_copy(ss2[:, :], rs[:, :]).then_inc(fin_step, 1)
                dve.wait_ge(fin_root, 1)
                vec.reciprocal(w, w).then_inc(fin_step, 1)
                dve.wait_ge(fin_step, 4)
                vec.tensor_tensor(rs[:, :], rs[:, :], w, ALU.mult).then_inc(fin_step, 1)
                dve.wait_ge(fin_step, 5)

            linear("C_qka", both_norms)
            for t in range(DT):
                vec.scalar_tensor_tensor(out=res[:, t, :], in0=res[:, t, :], scalar=gains[:, FINAL + t:FINAL + t + 1],
                                         in1=ss2[:, :], op0=ALU.mult, op1=ALU.mult).then_inc(fin_res, 1)
            for name in ("C_va", "C_qkb", "C_vb"):
                linear(name)
            dve.wait_ge(absd_ready, 1)
            vec.scalar_tensor_tensor(out=absd[:, :], in0=absd[:, :], scalar=-1.0, in1=absd[:, :],
                                     op0=ALU.mult, op1=ALU.min).then_inc(absd_scaled, 1)
            softmax("DA", yah, yal)
            softmax("NA", ybh, ybl)
            linear("C_merge")
            linear("C_out")

            norm_scale(5)
            dve.wait_ge(fin_res, DT)
            for t in range(DT + 1):
                if t >= 1:
                    dve.wait_ge(post_scaled, t)
                    vec.tensor_tensor(res[:, t - 1, :], res[:, t - 1, :], acc[:, t - 1, :], ALU.add).then_inc(sq_src, 1)
                if t < DT:
                    vec.scalar_tensor_tensor(out=acc[:, t, :], in0=acc[:, t, :],
                                             scalar=gains[:, POSTMIX + t:POSTMIX + t + 1],
                                             in1=rs[:, :], op0=ALU.mult, op1=ALU.mult).then_inc(post_scaled, 1)
                if t >= 1:
                    part_lo("post_mix", t - 1, res[:, t - 1:t, :])
            for t in range(DT):
                add_square(6, t, t % 4)
            feed_forward(2)
            dve.wait_ge(norm_root, 8)
            vec.reciprocal(rst[:, :, :], rst[:, :, :]).then_inc(tok_rs, 1)
            dve.wait_ge(tok_rs, 1)
            for i in range(2 * TT):
                t, a = divmod(i, 2)
                dve.wait_ge(ot_done, i + 1)
                r = result[:, t, 512 * a:512 * a + 512]
                vec.scalar_tensor_tensor(out=r, in0=psum[:, (5 + i) % 8, :], scalar=rst[:, t, 0:1], in1=r,
                                         op0=ALU.mult, op1=ALU.add).then_inc(ot_out, 1)

        @block.tensor
        def _(pe):
            mm = nc.tensor.matmul

            def three(out, a_hi, a_lo, b_hi, b_lo, start, stop):
                mm(out, a_hi, b_lo, start=start, stop=False)
                mm(out, a_lo, b_hi, start=False, stop=False)
                return mm(out, a_hi, b_hi, start=False, stop=stop)

            def ready(name):
                if name in ("A_qk", "A_v", "A_o"):
                    return n_lo, 0
                if name == "A_out":
                    return a_lo, 0
                if name[:2] == "up":
                    return n_lo, DT * {"0": 1, "1": 4, "2": 6}[name[2]]
                if name[:4] == "down":
                    return h_lo, st["up" + name[4:]].h0
                return {"B_k": (n_lo, DT * 2), "B_v": (n_lo, DT * 2), "B_q": (n_lo, DT * 3),
                        "B_out": (y_lo, att["B"].y0), "C_out": (m_lo, 0)}.get(name, (n_lo, DT * 5))

            def multiply(name, b, par, first, between=(None, None)):
                s = st[name]
                pe.wait_ge(w_lo, b + 1)
                if not isinstance(b, int) or b >= 2:
                    pe.wait_ge(block_out, b - 1)
                sem_, count = ready(name)
                inh, inl = {"down": (hidh, hidl), "store": (mgh, mgl)}.get(s.kind, (xh, xl))
                if name[:3] in ("up0", "up1"):
                    inh, inl = x2h, x2l
                kt = s.kt
                whp, wlp = wh[:, par], wl[:, par]
                if s.kind == "tokens":
                    for t in range(TT):
                        o = psum[:, 2 * par + t // 2, 256 * (t % 2):256 * (t % 2) + 256]
                        for k in range(kt):
                            if first and t == 0:
                                pe.wait_ge(sem_, count + k + 1)
                            last = three(o, inh[:, k, t * P:(t + 1) * P], inl[:, k, t * P:(t + 1) * P],
                                         whp[:, k * 256:(k + 1) * 256], wlp[:, k * 256:(k + 1) * 256],
                                         k == 0, k == kt - 1)
                elif s.kind == "down":
                    for k in range(kt):
                        if first:
                            pe.wait_ge(sem_, count + k + 1)
                        last = three(psum[:, 2 * par, :], whp[:, k * P:(k + 1) * P], wlp[:, k * P:(k + 1) * P],
                                     inh[:, k, :], inl[:, k, :], k == 0, k == kt - 1)
                else:
                    bank = first_bank(name, 0 if first else b, par)
                    order = [(a, k) for k in range(kt) for a in range(2)] if first else [
                        (a, k) for a in range(2) for k in range(kt)]
                    for a, k in order:
                        if first and a == 0:
                            if k == between[0]:
                                between[1]()
                            pe.wait_ge(sem_, count + k + 1)
                        c = (a * DT + k) * P if s.kind == "up" else k * 256 + a * P
                        last = three(psum[:, bank + a, :], whp[:, c:c + P], wlp[:, c:c + P],
                                     inh[:, k, :], inl[:, k, :], k == 0, k == kt - 1)
                last.then_inc(mm_done, 1)

            def merge(b, par, first=False):
                pe.wait_ge(w_lo, b + 1)
                pe.wait_ge(block_out, b - 1)
                if first and par == 1:
                    pe.wait_ge(y_lo, att["NA"].y0 + 4)
                bank = 4 if first and par == 0 else 2 * par
                kt = DT if par == 0 else 4
                for a in range(2):
                    inh, inl = (xh, xl) if par == 0 else ((yah, yal), (ybh, ybl))[a]
                    for k in range(kt):
                        c = (a * kt + k) * P
                        last = three(psum[:, bank + a, :], wh[:, par, c:c + P], wl[:, par, c:c + P],
                                     inh[:, k, :], inl[:, k, :], k == 0, k == kt - 1)
                last.then_inc(mm_done, 1)

            def linear(name, norm=None, between=(None, None)):
                s = st[name]
                if s.kind == "merge":
                    merge(s.b0, 0, True)
                    merge(s.b0 + 1, 1, True)
                    with nc.tensor.Fori(1, s.blocks // 2) as j:
                        merge(s.b0 + 2 * j, 0)
                        merge(s.b0 + 2 * j + 1, 1)
                    return
                multiply(name, s.b0, 0, True, between)
                if norm is not None:
                    norm_total(norm)
                multiply(name, s.b0 + 1, 1, False)
                if s.blocks == 4:
                    multiply(name, s.b0 + 2, 0, False)
                    multiply(name, s.b0 + 3, 1, False)
                elif s.blocks > 4:
                    with nc.tensor.Fori(1, s.blocks // 2) as j:
                        multiply(name, s.b0 + 2 * j, 0, False)
                        multiply(name, s.b0 + 2 * j + 1, 1, False)

            def norm_total(k):
                pe.wait_ge(ss_added, 8 * (k + 1))
                if k == 4:
                    pe.wait_ge(ss2_added, DT + 1)
                    mm(psum[:, 5, :], ones[:, :], ss2[:, :], start=True, stop=True)
                mm(psum[:, 4, :], ones[:, :], ss[:, :], start=True, stop=True).then_inc(norm_sum, 1)

            def turn(tensor, i, bank):
                t, a = divmod(i, 2)
                for k in range(4):
                    last = nc.tensor.transpose(psum[:, bank, k * P:(k + 1) * P],
                                               tensor[:, 4 * a + k, t * P:(t + 1) * P], ident[:, :])
                return last

            def feed_forward(f):
                linear(f"up{f}0", (1, 3, 6)[f])
                linear(f"down{f}0")
                if f == 2:
                    for i in range(2 * TT):
                        if i >= 2:
                            pe.wait_ge(rt_out, i - 1)
                        turn(res, i, 4 + i % 2).then_inc(rt_done, 1)
                linear(f"up{f}1")
                linear(f"down{f}1")

            def turn_rs(n):
                if n == 2:
                    pe.wait_ge(fin_step, 5)
                else:
                    pe.wait_ge(norm_rs, (1, 3)[n])
                for t in range(TT):
                    last = nc.tensor.transpose(psum[:, 6, t * 8:(t + 1) * 8], rs[0:8, t * P:(t + 1) * P], ident[0:8, 0:8])
                last.then_inc(rst_t, 1)

            def softmax(which, q_of, k_of, v_of):
                r = att[which]
                for t in range(r.units + r.lag + 4):
                    if t < r.units:
                        h, qt = divmod(t, TT)
                        for m in range(r.maps):
                            g = r.s0 + t * r.maps + m
                            if g >= 2:
                                pe.wait_ge(s_biased, g - 1)
                            mm(psum[:, 4 + g % 2, 0:r.keys(qt)], q_of(h, m)[:, qt * P:(qt + 1) * P],
                               k_of(h, m)[:, 0:r.keys(qt)], start=True, stop=True).then_inc(s_done, 1)
                    u = t - r.lag
                    if 0 <= u < r.units:
                        n = r.keys(u % TT) // P
                        pe.wait_ge(s_prob, r.u0 + u + 1)
                        if r.u0 + u >= 2:
                            pe.wait_ge(t_out, r.u0 + u - 1)
                        for k in range(n):
                            last = nc.tensor.transpose(psum[:, 6 + (r.u0 + u) % 2, k * P:(k + 1) * P],
                                                       row_buffer(which, u, 0, S)[:, k * P:(k + 1) * P], ident[:, :])
                        last.then_inc(t_done, 1)
                    u = t - r.lag - 1
                    if 0 <= u < r.units and u % TT == TT - 1:
                        h = u // TT
                        y = r.y0 + h // r.per_tile
                        pe.wait_ge(t_out, r.u0 + u + 1)
                        if y >= 2:
                            pe.wait_ge(y_lo, y - 1)
                        width = P // r.per_tile
                        rows = width * (h % r.per_tile)
                        for k in range(TT):
                            q0 = k * P if r.causal else 0
                            last = mm(psum[rows:rows + width, y % 2, q0:S], v_of(h, k), pt[:, h % 2, k, q0:S],
                                      start=(k == 0), stop=(k == TT - 1))
                        last.then_inc(pv_done, 1)
                    u = t - r.lag - 3
                    if which == "DA" and 0 <= u < r.units and u % TT == TT - 1:
                        y = r.y0 + u // TT
                        pe.wait_ge(d_sq, u // TT + 1)
                        mm(psum[:, 2 + y % 2, :], ones[:, :], datmp[:, 0, :], start=True, stop=True).then_inc(d_ss, 1)

            pe.wait_ge(const, 8)
            pe.wait_ge(x_in, 16 * TT)
            for k in range(DT):
                if k == 2:
                    pe.wait_ge(small_in, 16 * 18)
                    nc.tensor.transpose(psum[:, 7, 0:NGAIN], gload[0:NGAIN, :],
                                        ident[0:NGAIN, 0:NGAIN]).then_inc(gain_t, 1)
                if k >= 2:
                    pe.wait_ge(xt_out, k - 1)
                for t in range(TT):
                    last = nc.tensor.transpose(psum[:, 4 + k % 2, t * P:(t + 1) * P], xin[:, t, k * P:(k + 1) * P],
                                               ident[:, :])
                last.then_inc(xt_done, 1)
            pe.wait_ge(lam_step, 4)
            mm(psum[:, 6, 0:1], ones[0:1, :], lam[0:1, 4:5], start=True, stop=True).then_inc(lam_mm, 1)
            pe.wait_ge(wg_lo, 1)
            for k in range(DT):
                pe.wait_ge(n_lo, k + 1)
                last = three(psum[0:16, 7, :], wgh[:, k, :], wgl[:, k, :], xh[:, k, :], xl[:, k, :],
                             k == 0, k == DT - 1)
            last.then_inc(g_done, 1)
            linear("A_qk", 0)
            turn_rs(0)
            linear("A_v")
            linear("A_o")
            pe.wait_ge(g_step, 9)
            for t in range(TT):
                last = nc.tensor.transpose(psum[:, 6, t * A_HEADS:(t + 1) * A_HEADS], gu[:, t * P:(t + 1) * P],
                                           ident[0:A_HEADS, 0:A_HEADS])
            last.then_inc(u_t, 1)
            pe.wait_ge(block_out, st["A_o"].b0 + 4)
            pe.wait_ge(u_ready, 1)
            def scores(h, tiles):
                rows = slice(A_DQK * (h % 2), A_DQK * (h % 2) + A_DQK)
                for t in tiles:
                    g = TT * h + t
                    if g >= 2:
                        pe.wait_ge(a_p, g - 1)
                    mm(psum[:, 4 + g % 2, 0:S - t * P], qk[rows, 4 + h // 2, t * P:(t + 1) * P],
                       qk[rows, h // 2, t * P:S], start=True, stop=True).then_inc(a_s, 1)

            def head_squares(e):
                pe.wait_ge(a_sq, e + 1)
                mm(psum[:, 2 + e % 2, :], ones[:, :], hq[:, :], start=True, stop=True).then_inc(a_ss, 1)

            for h in range(A_HEADS + 1):
                if h < A_HEADS:
                    if h >= 1:
                        pe.wait_ge(a_d, TT * h)
                    mm(psum[:, 6, :], sel[:, h, :], gm[:, :], start=True, stop=True)
                    if h >= 1:
                        pe.wait_ge(a_floor, h)
                    mm(psum[:, 7, :], sel[:, h, :], gn[:, :], start=True, stop=True).then_inc(a_mrow, 1)
                    scores(h, (0, 1))
                if h >= 1:
                    e = h - 1
                    pe.wait_ge(a_p, TT * (e + 1))
                    if e >= 2:
                        pe.wait_ge(a_rs, e - 1)
                    for t in range(TT):
                        mm(psum[:, e % 2, t * P:S], va[:, t, e * A_DV:(e + 1) * A_DV], pt[:, e % 2, t, 0:S - t * P],
                           start=(t == 0), stop=(t == TT - 1))
                    if h >= 2:
                        head_squares(h - 2)
                    for t in range(TT):
                        last = mm(psum[:, 2 + e % 2, t * P:S], ones[:, :], pt[:, e % 2, t, 0:S - t * P],
                                  start=(t == 0), stop=(t == TT - 1))
                    last.then_inc(a_den, 1)
                if h < A_HEADS:
                    scores(h, (2, 3))
            linear("A_out", between=(3, lambda: head_squares(A_HEADS - 1)))
            feed_forward(0)
            linear("B_k", 2)
            turn_rs(1)
            linear("B_v")
            linear("B_q")
            pe.wait_ge(block_out, st["B_q"].b0 + 4)

            def half(tensor, h, tile0=0):
                return tensor[DH * (h % 2):DH * (h % 2) + DH, tile0 + h // 2, :]

            softmax("B", lambda h, m: half(bq, h), lambda h, m: half(bk, h),
                    lambda h, k: bv[:, k, h * DH:(h + 1) * DH])
            linear("B_out")
            feed_forward(1)
            linear("C_qka", 4)
            turn_rs(2)
            for name in ("C_va", "C_qkb", "C_vb"):
                linear(name)
            pe.wait_ge(block_out, st["C_vb"].b0 + 2)
            softmax("DA", lambda h, m: half(qk, 2 * h + m), lambda h, m: half(qk, 2 * h + m, 4),
                    lambda h, k: cva[:, k, h * P:(h + 1) * P])
            softmax("NA", lambda h, m: half(qkb, h), lambda h, m: half(qkb, h, 4),
                    lambda h, k: cvb[:, k, h * DH:(h + 1) * DH])
            linear("C_merge")
            linear("C_out")
            norm_total(5)
            feed_forward(2)
            pe.wait_ge(ss_added, 8 * 8)
            for t in range(TT):
                last = mm(psum[:, 4, t * 8:(t + 1) * 8], ss[:, t * P:(t + 1) * P], ones[:, 0:8], start=True, stop=True)
            last.then_inc(norm_sum, 1)
            pe.wait_ge(post_ready, DT)
            for i in range(2 * TT):
                if i == 2 * TT - 1:
                    pe.wait_ge(norm_root, 8)
                turn(post, i, (5 + i) % 8).then_inc(ot_done, 1)


_INS = ["x", "a_w_in", "a_b_gate", "a_g_head", "a_w_out", "b_w_q", "b_rel_bias", "b_w_o", "kv_norm_g", "w_kv",
        "norm_mix_g", "norm_ffn_g", "ffn_w_gate", "ffn_w_up", "ffn_w_down", "final_norm_g", "pre_mix_w_2", "w_in_2",
        "b_gate_2", "lambda_q1_2", "lambda_k1_2", "lambda_q2_2", "lambda_k2_2", "subln_w_2", "rpb_2",
        "w_branch_a_2", "w_branch_b_2", "w_out_2", "post_mix_w_2", "pre_ffn_w_2", "w_gate_2", "w_up_2", "w_down_2",
        "post_ffn_w_2"]


def kernel(**inputs):
    import concourse.bacc as _bacc
    import numpy as _np
    from concourse.bass_utils import run_bass_kernel_spmd as _run

    nc = _bacc.Bacc("TRN2", target_bir_lowering=False, num_devices=1)
    arrays, args = {}, []
    for name in _INS:
        a = _np.ascontiguousarray(inputs[name])
        arrays[f"in_{name}_dram"] = a
        args.append(nc.dram_tensor(f"in_{name}_dram", a.shape, mybir.dt.from_np(a.dtype), kind="ExternalInput").ap())
    args.append(nc.dram_tensor("out_dram", (1, S, D), F32, kind="ExternalOutput").ap())
    build(nc, *args)
    r = _run(nc, [arrays], core_ids=[0])
    return r.results[0]["out_dram"]
```
